# Optimizing a Trainium2 kernel written in Bass

```python
import jax, jax.numpy as jnp
from jax import lax
import numpy as np

D_MODEL = 1024
BATCH = 1
SEQ = 2048
DEPTH = 1

MIX_WIDTH = D_MODEL
WIDTH_A = MIX_WIDTH // 2
WIDTH_B = MIX_WIDTH - WIDTH_A
HEADS_A = 4
HEAD_DIM_A = WIDTH_A // HEADS_A
GROUPS_B = 4
CHUNK = 128
CONV_K = 3
PLE_DIM = 256
EPS = 1e-6
SPLITS = [WIDTH_A, WIDTH_A, WIDTH_A, WIDTH_B, WIDTH_B, WIDTH_B, WIDTH_B]
PROJ_WIDTH = sum(SPLITS)

kernel_name = "hybrid_sgu_shortconv_ple_trunk"

def rmsnorm(x, g):
    xf = x.astype(jnp.float32)
    y = xf * lax.rsqrt(jnp.mean(xf * xf, axis=-1, keepdims=True) + EPS)
    return (y * g.astype(jnp.float32)).astype(x.dtype)

def layernorm(x, g, b):
    xf = x.astype(jnp.float32)
    mu = jnp.mean(xf, axis=-1, keepdims=True)
    xc = xf - mu
    var = jnp.mean(xc * xc, axis=-1, keepdims=True)
    y = xc * lax.rsqrt(var + EPS)
    return (y * g.astype(jnp.float32) + b.astype(jnp.float32)).astype(x.dtype)

def spatial_gating(u, v, ln_g, ln_b, w_s, b_s):
    bsz, s_len, _ = v.shape
    n_chunks = s_len // CHUNK
    v = layernorm(v, ln_g, ln_b)
    vh = v.reshape(bsz, n_chunks, CHUNK, HEADS_A, HEAD_DIM_A)
    mask = jnp.tril(jnp.ones((CHUNK, CHUNK), dtype=w_s.dtype))
    ws = w_s * mask[None]
    mixed = jnp.einsum('hts,bnshd->bnthd', ws, vh)
    mixed = mixed + jnp.transpose(b_s)[None, None, :, :, None]
    return u * mixed.reshape(bsz, s_len, WIDTH_A)

def gated_short_conv(h, gate_b, gate_c, conv_w):
    s_len = h.shape[1]
    xc = gate_c * h
    xp = jnp.pad(xc, ((0, 0), (CONV_K - 1, 0), (0, 0)))
    y = xp[:, 0:s_len] * conv_w[:, 0]
    for k in range(1, CONV_K):
        y = y + xp[:, k:k + s_len] * conv_w[:, k]
    return gate_b * y

def setup_inputs(seed: int = 0) -> dict:
    key = jax.random.key(seed)
    ks = jax.random.split(key, 16)
    f32 = jnp.float32
    x = jax.random.normal(ks[0], (BATCH, SEQ, D_MODEL), f32)
    p = jax.random.normal(ks[1], (DEPTH, BATCH, SEQ, PLE_DIM), f32)
    norm_g = 1.0 + 0.02 * jax.random.normal(ks[2], (DEPTH, D_MODEL), f32)
    w_in = jax.random.normal(ks[3], (DEPTH, D_MODEL, PROJ_WIDTH), f32) * D_MODEL ** -0.5
    ln_v_g = 1.0 + 0.02 * jax.random.normal(ks[4], (DEPTH, WIDTH_A), f32)
    ln_v_b = 0.02 * jax.random.normal(ks[5], (DEPTH, WIDTH_A), f32)
    w_s = 0.5 * jax.random.normal(ks[6], (DEPTH, HEADS_A, CHUNK, CHUNK), f32) * CHUNK ** -0.5
    b_s = 1.0 + 0.1 * jax.random.normal(ks[7], (DEPTH, HEADS_A, CHUNK), f32)
    conv_w = jax.random.normal(ks[8], (DEPTH, WIDTH_B, CONV_K), f32) * CONV_K ** -0.5
    w_out = jax.random.normal(ks[9], (DEPTH, MIX_WIDTH, D_MODEL), f32) * MIX_WIDTH ** -0.5
    ple_norm_g = 1.0 + 0.02 * jax.random.normal(ks[10], (DEPTH, D_MODEL), f32)
    w_ple_gate = jax.random.normal(ks[11], (DEPTH, D_MODEL, D_MODEL), f32) * D_MODEL ** -0.5
    w_ple_proj = 0.5 * jax.random.normal(ks[12], (DEPTH, PLE_DIM, D_MODEL), f32) * PLE_DIM ** -0.5
    final_g = 1.0 + 0.02 * jax.random.normal(ks[13], (D_MODEL,), f32)
    return {"x": x, "p": p, "norm_g": norm_g, "w_in": w_in, "ln_v_g": ln_v_g,
            "ln_v_b": ln_v_b, "w_s": w_s, "b_s": b_s, "conv_w": conv_w,
            "w_out": w_out, "ple_norm_g": ple_norm_g, "w_ple_gate": w_ple_gate,
            "w_ple_proj": w_ple_proj, "final_g": final_g}

def reference(x, p, norm_g, w_in, ln_v_g, ln_v_b, w_s, b_s, conv_w, w_out,
              ple_norm_g, w_ple_gate, w_ple_proj, final_g):
    split_idx = list(np.cumsum(SPLITS)[:-1])
    for i in range(DEPTH):
        hn = rmsnorm(x, norm_g[i])
        proj = hn @ w_in[i]
        u_a, v_a, z_a, h_b, gb, gc, z_b = jnp.split(proj, split_idx, axis=-1)
        out_a = spatial_gating(u_a, v_a, ln_v_g[i], ln_v_b[i], w_s[i], b_s[i]) * jax.nn.silu(z_a)
        out_b = gated_short_conv(h_b, gb, gc, conv_w[i]) * jax.nn.silu(z_b)
        x = x + jnp.concatenate([out_a, out_b], axis=-1) @ w_out[i]
        gate = jax.nn.sigmoid(rmsnorm(x, ple_norm_g[i]) @ w_ple_gate[i])
        x = x + gate * (p[i] @ w_ple_proj[i])
    return rmsnorm(x, final_g)


_drawn_inputs = setup_inputs


def setup_inputs(seed=0):
    import zlib

    import numpy as np

    out = dict(_drawn_inputs(seed))
    spreads = {}
    factors = {'norm_g': 3.172,
     'ln_v_g': 64.0,
     'ln_v_b': 64.0,
     'ple_norm_g': 64.0,
     'final_g': 7.519,
     'p': 7.726,
     'b_s': 5.361,
     'w_ple_gate': 8.0,
     'w_ple_proj': 7.731}
    for name, (base, spread) in spreads.items():
        noise = np.random.default_rng([zlib.crc32(name.encode()), seed]).standard_normal(out[name].shape)
        drawn = base * np.exp(spread * noise) if base else spread * noise
        out[name] = __import__('jax').numpy.asarray(drawn.astype(out[name].dtype))
    for name, factor in factors.items():
        out[name] = (out[name] * factor).astype(out[name].dtype)
    return out
```

```python
from contextlib import ExitStack

import concourse.bass as bass
from concourse import mybir

P = 128
HALF = 512
F32 = mybir.dt.float32
F32R = mybir.dt.float32r
I32 = mybir.dt.int32
BF16 = mybir.dt.bfloat16
ALU = mybir.AluOpType
ACT = mybir.ActivationFunctionType
EPS = 1e-6
RSQRT_MAGIC = 0x5F3759DF
NEWTON_ROUNDS = 3

V0, T0, O0, G0, UNITS = 0, 4, 28, 36, 46
Q = 4 * UNITS
PARTS = ("z_a", "u", "h", "gate_c", "gate_b", "z_b")
O_CHUNKS = ((4, 5), (6, 7), (0, 1), (2, 3))


def unit_kind(u):
    if u < T0:
        return "V", 0, u
    if u < O0:
        return "T", (u - T0) // 6, (u - T0) % 6
    if u < G0:
        return "O", (u - O0) // 4, (u - O0) % 4
    half, part = divmod(u - G0, 5)
    return ("P", half, 0) if part == 0 else ("G", half, part - 1)


READERS = (["act"] * 4 + ["dve", "dve", "act", "dve", "dve", "dve"] * 4 + ["dve"] * 8 + ["act"] * 16)
ACC_BANKS = 6
ACT_READS = READERS.count("act")
DVE_READS = READERS.count("dve")


def acc_index(u, tile):
    kind, a, part = unit_kind(u)
    if kind == "V":
        return tile
    if kind == "T":
        return u
    if kind == "O":
        return 28 + 4 * a + tile
    return 36 + 8 * a + (4 if kind == "G" else 0) + tile


def reads_through(n):
    return READERS[:n + 1].count(READERS[n])


JOBS_AFTER = {
    27: [("mix", 0, 0), ("mix", 1, 0)],
    28: [("mix", 2, 0), ("mix", 3, 0)],
    29: [("xt", 0, 0), ("xt", 0, 1)],
    30: [("pt", 0, 0), ("pt", 1, 0)],
    31: [("xt", 1, 0), ("xt", 1, 1)],
    32: [("x1t", 0, 0), ("x1t", 1, 0)],
    33: [("x1t", 2, 0), ("x1t", 3, 0)],
    36: [("x1t", 0, 1), ("x1t", 1, 1)],
    37: [("x1t", 2, 1), ("x1t", 3, 1)],
    39: [("xt", 2, 0), ("xt", 2, 1)],
    41: [("xt", 3, 0), ("xt", 3, 1)],
}
JOBS = sum(len(v) for v in JOBS_AFTER.values())
PRO_JOBS = 10


def jobs_of(last):
    return [(u, job) for u in sorted(JOBS_AFTER) for job in JOBS_AFTER[u] if not (last and job[0] == "xt")]


def build(nc, x, p, norm_g, w_in, ln_v_g, ln_v_b, w_s, b_s, conv_w, w_out, ple_norm_g, w_ple_gate,
          w_ple_proj, final_g, out):
    _, seq, d = x.shape
    width = ln_v_g.shape[1]
    heads, chunk = b_s.shape[1], b_s.shape[2]
    ple = p.shape[3]
    KC = d // P
    TILES = HALF // P
    BLOCKS = seq // HALF
    KP = ple // P
    assert (KC, TILES, heads, chunk, width, KP) == (8, 4, 4, P, HALF, 2)
    COLUMN0 = {"u": 0, "v": width, "z_a": 2 * width, "h": 3 * width, "gate_b": 4 * width,
               "gate_c": 5 * width, "z_b": 6 * width}

    x_tiles = x[0].rearrange("(b i p) d -> b i p d", i=TILES, p=P)
    x_block = x[0].rearrange("(b i p) d -> b p i d", i=TILES, p=P)
    p_block = p[0, 0].rearrange("(b i p) c -> b p i c", i=TILES, p=P)
    out_tiles = out[0].rearrange("(b i p) d -> b i p d", i=TILES, p=P)
    w_in_k = w_in[0].rearrange("(k p) n -> p k n", p=P)
    w_out_k = w_out[0].rearrange("(k p) n -> p k n", p=P)
    w_gate_k = w_ple_gate[0].rearrange("(k p) n -> p k n", p=P)
    w_proj_k = w_ple_proj[0].rearrange("(k p) n -> p k n", p=P)

    with ExitStack() as ctx:
        def sb(name, shape, dt):
            return ctx.enter_context(nc.sbuf_tensor(name, shape, dt))

        def sem(name):
            return ctx.enter_context(nc.semaphore(name))

        hn_hi = sb("hn_hi", [P, KC, HALF], F32R)
        hn_lo = sb("hn_lo", [P, KC, HALF], F32R)
        mix_hi = sb("mix_hi", [P, KC, HALF], F32R)
        mix_lo = sb("mix_lo", [P, KC, HALF], F32R)
        x1_hi = sb("x1_hi", [P, KC, HALF], F32R)
        x1_lo = sb("x1_lo", [P, KC, HALF], F32R)
        pt_hi = sb("pt_hi", [P, KP, HALF], F32R)
        pt_lo = sb("pt_lo", [P, KP, HALF], F32R)
        wst_hi = sb("wst_hi", [P, heads, P], F32R)
        wst_lo = sb("wst_lo", [P, heads, P], F32R)
        w_hi = sb("w_hi", [P, 2, 2 * HALF], F32R)
        w_lo = sb("w_lo", [P, 2, 2 * HALF], F32R)
        ones_r = sb("ones_r", [P, P], F32R)

        w_raw = sb("w_raw", [P, 2, 2 * HALF], F32)
        x_in = sb("x_in", [P, 2, d], F32)
        x_res = sb("x_res", [P, TILES, d], F32)
        norm_b = sb("norm_b", [P, d], F32)
        final_b = sb("final_b", [P, d], F32)
        uz = sb("uz", [P, TILES, HALF], F32)
        v_raw = sb("v_raw", [P, TILES, HALF], F32)
        mix_add = sb("mix_add", [P, heads, P], F32)
        p_nat = sb("p_nat", [P, TILES, ple], F32)
        ident = sb("ident", [P, P], F32)
        xc = sb("xc", [P, HALF + 2], F32)
        xc_tail = sb("xc_tail", [P, heads, 2], F32)
        conv = sb("conv", [P, HALF], F32)
        h_copy = sb("h_copy", [P, HALF], F32)
        gate = sb("gate", [P, 2, HALF], F32)
        branch = sb("branch", [P, 2, HALF], F32)
        square = sb("square", [P, d], BF16)
        ln_g_c = sb("ln_g_c", [P, heads], F32)
        ln_b_c = sb("ln_b_c", [P, heads], F32)
        conv_c = sb("conv_c", [P, heads, 3], F32)
        ple_c = sb("ple_c", [P, KC], F32)
        bn = sb("bn", [P, TILES, 6], F32)
        mean_var = sb("mean_var", [P, TILES, 2], F32)
        sums = sb("sums", [P, 16], F32)
        half_var = sb("half_var", [P, 16], F32)
        var = sb("var", [P, 16], F32)
        shifted = sb("shifted", [P, 16], I32)
        rstd = sb("rstd", [P, 16], F32)
        newton = sb("newton", [P, 16], F32)
        warm = sb("warm", [P, 2], F32)
        three_halves = sb("three_halves", [P, 16], F32)
        C_V, C_X, C_X1, C_X2 = 0, 4, 8, 12

        acc = ctx.enter_context(nc.psum_tensor("acc", [P, ACC_BANKS, HALF], F32))
        small = ctx.enter_context(nc.psum_tensor("small", [P, 2, HALF], F32))

        w_landed = [sem("w_landed0"), sem("w_landed1")]
        x_in_landed = [sem("x_in_landed0"), sem("x_in_landed1")]
        x_res_landed = sem("x_res_landed")
        p_landed = sem("p_landed")
        norm_landed = sem("norm_landed")
        const_landed = sem("const_landed")
        out_stored = sem("out_stored")
        quarters = sem("quarters")
        mix_done = sem("mix_done")
        xt_done = sem("xt_done")
        pt_done = sem("pt_done")
        x1t_done = sem("x1t_done")
        wst_done = sem("wst_done")
        w_hi_ready = sem("w_hi_ready")
        acc_read_act = sem("acc_read_act")
        sigmoid_ready = sem("sigmoid_ready")
        branch_hi_ready = sem("branch_hi_ready")
        v_hi_ready = sem("v_hi_ready")
        small_hi_ready = sem("small_hi_ready")
        squares_done = sem("squares_done")
        w_lo_ready = sem("w_lo_ready")
        acc_read_dve = sem("acc_read_dve")
        small_read = sem("small_read")
        v_norm_ready = sem("v_norm_ready")
        v_lo_ready = sem("v_lo_ready")
        branch_ready = sem("branch_ready")
        branch_lo_ready = sem("branch_lo_ready")
        xn_ready = sem("xn_ready")
        x2_ready = sem("x2_ready")
        y_ready = sem("y_ready")
        seed_ready = sem("seed_ready")
        vec_step = sem("vec_step")
        ident_ready = sem("ident_ready")
        masked = sem("masked")
        newton_step = sem("newton_step")
        rstd_ready = sem("rstd_ready")
        pool_set = sem("pool_set")

        VEC_PRO, VEC_BLOCK = 7, 50
        EVENTS_PRO, EVENTS = 2, 4

        block = ctx.enter_context(nc.Block())

        def w_source(u):
            kind, a, part = unit_kind(u % UNITS)
            if kind == "V":
                return w_in_k[:, 2 * part:2 * part + 2, COLUMN0["v"]:COLUMN0["v"] + HALF]
            if kind == "T":
                c = COLUMN0[PARTS[part]] + a * P
                return w_in_k[:, :, c:c + P]
            cols = slice(a * HALF, (a + 1) * HALF)
            if kind == "O":
                k = O_CHUNKS[part][0]
                return w_out_k[:, k:k + 2, cols]
            if kind == "P":
                return w_proj_k[:, :, cols]
            return w_gate_k[:, 2 * part:2 * part + 2, cols]

        def w_view(t, u):
            k = KC if unit_kind(u % UNITS)[0] == "T" else 2
            return t[:, u % 2, :].rearrange("p (k n) -> p k n", k=k)

        def quarter(b, u, tile=3):
            return b * Q + 4 * u + tile + 1

        def event(b, e):
            return b * EVENTS + EVENTS_PRO + e + 1

        def over_blocks(eng, body):
            with eng.Fori(0, BLOCKS - 1) as b:
                body(b, False)
            body(BLOCKS - 1, True)

        @block.sync
        def _(sp):
            def load_w(b, u):
                if not (isinstance(b, int) and b == 0 and u < 2):
                    sp.wait_ge(w_lo_ready, b * UNITS + u - 1)
                sp.dma_start(w_view(w_raw, u), w_source(u)).then_inc(w_landed[u % 2], 16)

            sp.sem_inc(out_stored, 16 * TILES)
            sp.dma_start(x_in[:, 0, :], x_tiles[0, 0]).then_inc(x_in_landed[0], 16)
            load_w(0, 0)
            sp.dma_start(norm_b[:, :], norm_g[0:1, :].to_broadcast([P, d])).then_inc(norm_landed, 16)
            sp.dma_start(x_in[:, 1, :], x_tiles[0, 1]).then_inc(x_in_landed[1], 16)
            load_w(0, 1)
            for i in (2, 3):
                sp.wait_ge(xt_done, 2 * (i - 1))
                sp.dma_start(x_in[:, i % 2, :], x_tiles[0, i]).then_inc(x_in_landed[i % 2], 16)

            for u in range(2, 5):
                load_w(0, u)

            def body(b, last):
                for u in range(5, UNITS if last else UNITS + 5):
                    load_w(b, u)
                    if u == 12:
                        sp.wait_ge(out_stored, (b + 1) * (16 * TILES))
                        sp.dma_start(x_res[:, :, :], x_block[b]).then_inc(x_res_landed, 16)
                        sp.wait_ge(xt_done, b * 8 + 8)
                        sp.dma_start(p_nat[:, :, :], p_block[b]).then_inc(p_landed, 16)
                    if u == 5 and not last:
                        for i in (0, 1):
                            sp.wait_ge(xt_done, b * 8 + 6 + 2 * i)
                            sp.dma_start(x_in[:, i, :], x_tiles[b + 1, i]).then_inc(x_in_landed[i], 16)
                    if u in (31, 33) and not last:
                        i = 2 if u == 31 else 3
                        sp.wait_ge(xt_done, b * 8 + 8 + 2 * (i - 1))
                        sp.dma_start(x_in[:, i % 2, :], x_tiles[b + 1, i]).then_inc(x_in_landed[i % 2], 16)
                for i in range(TILES):
                    sp.wait_ge(y_ready, b * TILES + i + 1)
                    sp.dma_start(out_tiles[b, i], x_res[:, i, :]).then_inc(out_stored, 16)

            over_blocks(sp, body)
            sp.wait_ge(out_stored, (BLOCKS + 1) * TILES * 16)

        @block.gpsimd
        def _(pool):
            pool.memset(warm[:, 0:1], 0.0).then_inc(pool_set, 1)
            pool.memset(ident[:, :], 0.0).then_inc(pool_set, 1)
            pool.memset(three_halves[:, :], 1.5).then_inc(pool_set, 1)
            pool.memset(xc_tail[:, :, :], 0.0).then_inc(pool_set, 1)
            pool.wait_ge(pool_set, 4)
            pool.affine_select(out=ident[:, :], in_=ident[:, :], compare_op=ALU.not_equal, fill=1.0, base=0,
                               pattern=[[-1, P]], channel_multiplier=1).then_inc(ident_ready, 1)

            def rsqrt(b, e, cols):
                y, hv, t, c = (m[:, cols] for m in (rstd, half_var, newton, three_halves))
                n = b * EVENTS + (e if e < 0 else EVENTS_PRO + e) if e >= 0 else EVENTS_PRO + e
                per = 4 * NEWTON_ROUNDS - 1
                done = n * per
                pool.wait_ge(seed_ready, n + 1)
                for r in range(NEWTON_ROUNDS):
                    for s, (o, i0, i1, op) in enumerate(((t, y, y, ALU.mult), (t, t, hv, ALU.mult),
                                                         (t, c, t, ALU.subtract), (y, y, t, ALU.mult))):
                        if r or s:
                            pool.wait_ge(newton_step, done + 4 * r + s)
                        ins = pool.tensor_tensor(o, i0, i1, op)
                        if 4 * r + s < per:
                            ins.then_inc(newton_step, 1)
                        else:
                            ins.then_inc(rstd_ready, 1)

            rsqrt(0, -2, slice(C_X, C_X + 2))
            pool.wait_ge(const_landed, 16 * 7)
            wsn = uz[:, 0, :].rearrange("t (h s) -> t h s", h=heads)
            pool.affine_select(out=wsn, in_=wsn, compare_op=ALU.is_ge, fill=0.0, base=0,
                               pattern=[[0, heads], [-1, P]], channel_multiplier=1).then_inc(masked, 1)
            rsqrt(0, -1, slice(C_X + 2, C_X + 4))

            def body(b, last):
                rsqrt(b, 0, slice(C_V, C_V + (4 if last else 6)))
                if not last:
                    rsqrt(b, 1, slice(C_X + 2, C_X + 4))
                rsqrt(b, 1 if last else 2, slice(C_X1, C_X1 + 4))
                rsqrt(b, 2 if last else 3, slice(C_X2, C_X2 + 4))

            over_blocks(pool, body)

        @block.tensor
        def _(pe):
            def product(ps, left_hi, left_lo, right_hi, right_lo, first, last):
                pe.matmul(ps, left_hi, right_hi, start=first, stop=False)
                pe.matmul(ps, left_hi, right_lo, start=False, stop=False)
                return pe.matmul(ps, left_lo, right_hi, start=False, stop=last)

            def wait_bank(b, n):
                if n >= ACC_BANKS:
                    m = n - ACC_BANKS
                    if READERS[m] == "act":
                        pe.wait_ge(acc_read_act, b * ACT_READS + ACT_READS + reads_through(m))
                    else:
                        pe.wait_ge(acc_read_dve, b * DVE_READS + reads_through(m))
                else:
                    m = max(i for i in range(len(READERS)) if i % ACC_BANKS == n)
                    pe.wait_ge(acc_read_act, b * ACT_READS + reads_through(m))

            def unit(b, u):
                kind, a, part = unit_kind(u)
                pe.wait_ge(w_lo_ready, b * UNITS + u + 1)
                hi, lo = w_view(w_hi, u), w_view(w_lo, u)
                if kind == "T":
                    n = acc_index(u, 0)
                    wait_bank(b, n)
                    for k in range(KC):
                        ins = product(acc[:, n % ACC_BANKS, :], hi[:, k, :], lo[:, k, :],
                                      hn_hi[:, k, :], hn_lo[:, k, :], k == 0, k == KC - 1)
                        if k % 2:
                            ins.then_inc(quarters, 1)
                    return
                left_hi, left_lo, k0, first, last = {
                    "V": (hn_hi, hn_lo, 2 * part, part == 0, part == 3),
                    "O": (mix_hi, mix_lo, O_CHUNKS[part][0], part == 0, part == 3),
                    "P": (pt_hi, pt_lo, 0, True, True),
                    "G": (x1_hi, x1_lo, 2 * part, part == 0, part == 3),
                }[kind]
                for i in range(TILES):
                    n = acc_index(u, i)
                    if first:
                        wait_bank(b, n)
                    for kk in range(2):
                        k, t = k0 + kk, slice(i * P, (i + 1) * P)
                        ins = product(acc[:, n % ACC_BANKS, :], left_hi[:, k, t], left_lo[:, k, t],
                                      hi[:, kk, :], lo[:, kk, :], first and kk == 0, last and kk == 1)
                    ins.then_inc(quarters, 1)

            def transposes(bank, sources, done):
                for n, s in enumerate(sources):
                    ins = pe.transpose(small[:, bank, n * P:(n + 1) * P], s, ident[:, :])
                ins.then_inc(done, 1)

            def xt(i, half):
                transposes(half, [x_in[:, i % 2, (4 * half + k) * P:(4 * half + k + 1) * P] for k in range(4)], xt_done)

            pe.wait_ge(ident_ready, 1)
            for i in range(TILES):
                pe.wait_ge(xn_ready, i + 1)
                for half in range(2):
                    if i:
                        pe.wait_ge(small_read, 2 * i + half - 1)
                    xt(i, half)
            pe.wait_ge(masked, 1)
            pe.wait_ge(small_read, 7)
            transposes(0, [uz[:, 0, h * P:(h + 1) * P] for h in range(heads)], wst_done)
            pe.wait_ge(small_read, 9)
            pe.matmul(small[:, 1, :], ones_r[:, :], wst_hi[:, :, :], start=True, stop=False)
            pe.matmul(small[:, 1, :], ones_r[:, :], wst_lo[:, :, :], start=False, stop=True).then_inc(wst_done, 1)

            def body(b, last):
                index = {job: n for n, (_, job) in enumerate(jobs_of(last))}

                def small_count(job):
                    return b * JOBS + PRO_JOBS + index[job] + 1

                for u in range(UNITS):
                    kind, a, part = unit_kind(u)
                    if u == V0:
                        if last:
                            pe.wait_ge(small_read, (b - 1) * JOBS + PRO_JOBS + JOBS)
                        else:
                            pe.wait_ge(small_read, b * JOBS + PRO_JOBS - 2)
                    if kind == "O" and a == 0:
                        pe.wait_ge(branch_lo_ready, b * 8 + 2 * (part + 1))
                    if kind == "P" and a == 0:
                        pe.wait_ge(small_read, small_count(("pt", 1, 0)))
                    if kind == "G" and a == 0 and part in (0, 2):
                        pe.wait_ge(small_read, small_count(("x1t", 3, part // 2)))
                    unit(b, u)
                    for job in JOBS_AFTER.get(u, ()):
                        if job not in index:
                            continue
                        what, i, half = job
                        n = index[job]
                        pe.wait_ge(small_read, b * JOBS + PRO_JOBS + n - 1)
                        if what == "mix":
                            pe.wait_ge(v_lo_ready, b * TILES + TILES)
                            for c in range(TILES):
                                hs = slice(i * P, (i + 1) * P)
                                ins = product(small[:, n % 2, c * P:(c + 1) * P], x1_hi[:, c, hs], x1_lo[:, c, hs],
                                              wst_hi[:, i, :], wst_lo[:, i, :], True, True)
                            ins.then_inc(mix_done, 1)
                        elif what == "xt":
                            pe.wait_ge(xn_ready, b * TILES + TILES + i + 1)
                            xt_bank = n % 2
                            transposes(xt_bank, [x_in[:, i % 2, (4 * half + k) * P:(4 * half + k + 1) * P]
                                                 for k in range(4)], xt_done)
                        elif what == "pt":
                            pe.wait_ge(p_landed, b * 16 + 16)
                            transposes(n % 2, [p_nat[:, t, i * P:(i + 1) * P] for t in range(TILES)], pt_done)
                        else:
                            pe.wait_ge(acc_read_dve, b * DVE_READS + reads_through(28 + 4 * half + i))
                            transposes(n % 2, [x_res[:, i, (4 * half + k) * P:(4 * half + k + 1) * P]
                                               for k in range(4)], x1t_done)

            over_blocks(pe, body)

        @block.scalar
        def _(act):
            act.sem_inc(acc_read_act, ACT_READS)
            act.dma_start(uz[:, 0, :].rearrange("t (h s) -> t h s", h=heads),
                          w_s[0].rearrange("h t s -> t h s")).then_inc(const_landed, 16)
            act.dma_start(uz[:, 1, :], b_s.rearrange("l h t -> l (h t)").to_broadcast([P, heads * P])).then_inc(const_landed, 16)
            with nc.allow_non_contiguous_dma(reason="a few hundred parameters, once"):
                act.dma_start(ln_g_c[:, :], ln_v_g[0].rearrange("(h p) -> p h", p=P)).then_inc(const_landed, 16)
                act.dma_start(ln_b_c[:, :], ln_v_b[0].rearrange("(h p) -> p h", p=P)).then_inc(const_landed, 16)
                act.dma_start(conv_c[:, :, :], conv_w[0].rearrange("(h p) k -> p h k", p=P)).then_inc(const_landed, 16)
                act.dma_start(ple_c[:, :], ple_norm_g[0].rearrange("(k p) -> p k", p=P)).then_inc(const_landed, 16)
            act.dma_start(final_b[:, :], final_g.rearrange("(l n) -> l n", l=1).to_broadcast([P, d])).then_inc(const_landed, 16)

            def sigmoid_table():
                act.activation(warm[:, 1:2], warm[:, 0:1], ACT.Sigmoid)

            def split_hi(b, u):
                act.wait_ge(w_landed[u % 2], (b * (UNITS // 2) + u // 2 + 1) * 16)
                if not (isinstance(b, int) and b == 0 and u < 2):
                    act.wait_ge(quarters, b * Q + 4 * (u - 1))
                if unit_kind(u % UNITS)[0] == "G":
                    k = 2 * unit_kind(u)[2]
                    for kk in range(2):
                        ins = act.activation(w_view(w_hi, u)[:, kk, :], w_view(w_raw, u)[:, kk, :], ACT.Copy,
                                             scale=ple_c[:, k + kk:k + kk + 1])
                else:
                    ins = act.activation(w_hi[:, u % 2, :], w_raw[:, u % 2, :], ACT.Copy)
                ins.then_inc(w_hi_ready, 1)

            def squares(source, col, done):
                if done is not None:
                    act.wait_ge(squares_done, done)
                act.activation(square[:, :], source, ACT.Square, accum_out=sums[:, col:col + 1]).then_inc(squares_done, 1)

            def small_hi(bank, target):
                k = target.shape[1]
                act.activation(target, small[:, bank, :].rearrange("p (k n) -> p k n", k=k),
                               ACT.Copy).then_inc(small_hi_ready, 1)

            def hn_part(t, i, half):
                return t[:, 4 * half:4 * half + 4, i * P:(i + 1) * P]

            act.wait_ge(pool_set, 1)
            sigmoid_table()
            for i in (0, 1):
                act.wait_ge(x_in_landed[i], 16)
                squares(x_in[:, i, :], C_X + i, i or None)
            split_hi(0, 0)
            for i in (0, 1):
                for half in range(2):
                    act.wait_ge(xt_done, 2 * i + half + 1)
                    small_hi(half, hn_part(hn_hi, i, half))
            for i in (2, 3):
                act.wait_ge(x_in_landed[i % 2], 32)
                squares(x_in[:, i % 2, :], C_X + i, i)
            split_hi(0, 1)
            for i in (2, 3):
                for half in range(2):
                    act.wait_ge(xt_done, 2 * i + half + 1)
                    small_hi(half, hn_part(hn_hi, i, half))
            act.wait_ge(wst_done, 1)
            small_hi(0, wst_hi[:, :, :])
            for u in range(2, 5):
                split_hi(0, u)

            PRO_HI, HI_JOBS = 9, JOBS - heads

            def body(b, last):
                jobs = jobs_of(last)
                sigmoid_table()
                for slot in range(4, 50):
                    if not last or slot + 1 < UNITS:
                        split_hi(b, slot + 1)
                    kind, a, part = unit_kind(slot - 1) if slot <= UNITS else ("end", 0, 0)
                    if slot == 4:
                        for i in range(TILES):
                            act.wait_ge(quarters, quarter(b, 3, i))
                            act.activation(v_raw[:, i, :], acc[:, acc_index(3, i) % ACC_BANKS, :], ACT.Copy).then_inc(acc_read_act, 1)
                        if not last:
                            for i in (0, 1):
                                act.wait_ge(x_in_landed[i], (b * 2 + 3) * 16)
                                squares(x_in[:, i, :], C_X + i, b * 12 + 4 + i)
                    if kind == "T":
                        bank = acc[:, acc_index(slot - 1, 0) % ACC_BANKS, :]
                        what = PARTS[part]
                        if what in ("z_a", "z_b"):
                            g = 0 if what == "z_a" else 1
                            act.wait_ge(quarters, quarter(b, slot - 1))
                            if a:
                                if g == 0:
                                    act.wait_ge(acc_read_dve, b * DVE_READS + 5 * (a - 1) + 2)
                                else:
                                    act.wait_ge(branch_ready, b * 8 + a)
                            act.activation(gate[:, g, :], bank, ACT.Sigmoid).then_inc(sigmoid_ready, 1)
                        if what == "u":
                            act.wait_ge(v_norm_ready, b * TILES + a + 1)
                            act.activation(x1_hi[:, a, :], v_raw[:, a, :], ACT.Copy).then_inc(v_hi_ready, 1)
                        if what == "h":
                            act.wait_ge(quarters, quarter(b, slot - 1))
                            if a:
                                act.wait_ge(acc_read_dve, b * DVE_READS + 5 * (a - 1) + 3)
                            act.activation(h_copy[:, :], bank, ACT.Copy).then_inc(acc_read_act, 1)
                        if what == "z_b":
                            act.wait_ge(branch_ready, b * 8 + a + 1)
                            act.activation(mix_hi[:, 4 + a, :], branch[:, a % 2, :], ACT.Copy).then_inc(branch_hi_ready, 1)
                    if kind == "P":
                        for i in range(TILES):
                            act.wait_ge(quarters, quarter(b, slot - 1, i))
                            if a:
                                act.wait_ge(x2_ready, b * 8 + i + 1)
                            act.activation(uz[:, i, :], acc[:, acc_index(slot - 1, i) % ACC_BANKS, :],
                                           ACT.Copy).then_inc(acc_read_act, 1)
                    if kind == "G" and part == 3:
                        if a == 0:
                            act.wait_ge(rstd_ready, event(b, 1 if last else 2))
                        for i in range(TILES):
                            act.wait_ge(quarters, quarter(b, slot - 1, i))
                            if 4 * a + i >= 2:
                                act.wait_ge(x2_ready, b * 8 + 4 * a + i - 1)
                            act.activation(gate[:, i % 2, :], acc[:, acc_index(slot - 1, i) % ACC_BANKS, :],
                                           ACT.Sigmoid, scale=rstd[:, C_X1 + i:C_X1 + i + 1]).then_inc(acc_read_act, 1)
                    for n, (u, (what, i, half)) in enumerate(jobs):
                        if u != slot - 1:
                            continue
                        if what == "mix":
                            act.wait_ge(branch_ready, b * 8 + 4 + i + 1)
                            act.activation(mix_hi[:, i, :], branch[:, i % 2, :], ACT.Copy).then_inc(branch_hi_ready, 1)
                        elif what == "xt":
                            act.wait_ge(xt_done, b * 8 + 8 + 2 * i + half + 1)
                            small_hi(n % 2, hn_part(hn_hi, i, half))
                        elif what == "pt":
                            act.wait_ge(pt_done, b * KP + i + 1)
                            small_hi(n % 2, pt_hi[:, i:i + 1, :])
                        else:
                            act.wait_ge(x1t_done, b * 8 + 4 * half + i + 1)
                            small_hi(n % 2, hn_part(x1_hi, i, half))
                    if slot == 34 and not last:
                        for i in (2, 3):
                            act.wait_ge(x_in_landed[i % 2], (b * 2 + 4) * 16)
                            squares(x_in[:, i % 2, :], C_X + i, b * 12 + 4 + i)
                    if slot == 37:
                        for i in range(TILES):
                            act.wait_ge(acc_read_dve, b * DVE_READS + 25 + i)
                            squares(x_res[:, i, :], C_X1 + i, b * 12 + 4 + (0 if last else 4) + i)
                    if slot == 47:
                        for i in range(TILES):
                            act.wait_ge(x2_ready, b * 8 + 4 + i + 1)
                            squares(x_res[:, i, :], C_X2 + i, b * 12 + 4 + (4 if last else 8) + i)

            over_blocks(act, body)

        @block.vector
        def _(dve):
            steps = [0]

            def mark(ins):
                steps[0] += 1
                ins.then_inc(vec_step, 1)

            def step(b, ins):
                mark(ins)
                wait_steps(b)

            def wait_steps(b):
                if b is None:
                    dve.wait_ge(vec_step, steps[0])
                else:
                    dve.wait_ge(vec_step, b * VEC_BLOCK + VEC_PRO + steps[0])

            def split_lo(b, u):
                dve.wait_ge(w_hi_ready, b * UNITS + u + 1)
                if unit_kind(u % UNITS)[0] == "G":
                    k = 2 * unit_kind(u)[2]
                    for kk in range(2):
                        ins = dve.scalar_tensor_tensor(
                            out=w_view(w_lo, u)[:, kk, :], in0=w_view(w_raw, u)[:, kk, :],
                            scalar=ple_c[:, k + kk:k + kk + 1], in1=w_view(w_hi, u)[:, kk, :].bitcast(F32),
                            op0=ALU.mult, op1=ALU.subtract)
                else:
                    ins = dve.tensor_tensor(w_lo[:, u % 2, :], w_raw[:, u % 2, :],
                                            w_hi[:, u % 2, :].bitcast(F32), ALU.subtract)
                ins.then_inc(w_lo_ready, 1)

            def small_lo(bank, hi, lo):
                k = lo.shape[1]
                dve.tensor_tensor(lo, small[:, bank, :].rearrange("p (k n) -> p k n", k=k),
                                  hi.bitcast(F32), ALU.subtract).then_inc(small_read, 1)

            def hn_part(t, i, half):
                return t[:, 4 * half:4 * half + 4, i * P:(i + 1) * P]

            def mean_squares(b, c0, c1):
                step(b, dve.tensor_scalar(var[:, c0:c1], sums[:, c0:c1], 1.0 / d, EPS, ALU.mult, ALU.add))

            def first_guess(b, c0, c1):
                step(b, dve.tensor_scalar(half_var[:, c0:c1], var[:, c0:c1], 0.5, None, ALU.mult))
                step(b, dve.tensor_scalar(shifted[:, c0:c1], var[:, c0:c1].bitcast(I32), 1, None,
                                          ALU.logical_shift_right))
                dve.tensor_scalar(rstd[:, c0:c1].bitcast(I32), shifted[:, c0:c1], -1.0, float(RSQRT_MAGIC),
                                  ALU.mult, ALU.add).then_inc(seed_ready, 1)

            def normalise_x(i):
                dve.scalar_tensor_tensor(out=x_in[:, i % 2, :], in0=x_in[:, i % 2, :],
                                         scalar=rstd[:, C_X + i:C_X + i + 1], in1=norm_b[:, :],
                                         op0=ALU.mult, op1=ALU.mult).then_inc(xn_ready, 1)

            step(None, dve.memset(ones_r[:, :].bitcast(F32), 1.0))
            for pair in range(2):
                dve.wait_ge(squares_done, 2 * pair + 2)
                mean_squares(None, C_X + 2 * pair, C_X + 2 * pair + 2)
                first_guess(None, C_X + 2 * pair, C_X + 2 * pair + 2)
                if pair == 0:
                    dve.wait_ge(norm_landed, 16)
                dve.wait_ge(w_hi_ready, pair + 1)
                split_lo(0, pair)
                dve.wait_ge(rstd_ready, pair + 1)
                for i in (2 * pair, 2 * pair + 1):
                    normalise_x(i)
                for i in (2 * pair, 2 * pair + 1):
                    for half in range(2):
                        dve.wait_ge(small_hi_ready, 2 * i + half + 1)
                        small_lo(half, hn_part(hn_hi, i, half), hn_part(hn_lo, i, half))
            dve.wait_ge(small_hi_ready, 9)
            small_lo(0, wst_hi[:, :, :], wst_lo[:, :, :])
            for u in range(2, 5):
                split_lo(0, u)
                if u == 2:
                    dve.wait_ge(wst_done, 2)
                    dve.wait_ge(const_landed, 16 * 7)
                    for h in range(heads):
                        ins = dve.scalar_tensor_tensor(
                            out=mix_add[:, h, :], in0=small[:, 1, h * P:(h + 1) * P], scalar=ln_b_c[:, h:h + 1],
                            in1=uz[:, 1, h * P:(h + 1) * P], op0=ALU.mult, op1=ALU.add)
                    ins.then_inc(small_read, 1)
            assert steps[0] == VEC_PRO

            PRO_HI, HI_JOBS = 9, JOBS - heads

            def body(b, last):
                steps[0] = 0
                jobs = jobs_of(last)
                for slot in range(4, 50):
                    if not last or slot + 1 < UNITS:
                        split_lo(b, slot + 1)
                    kind, a, part = unit_kind(slot - 1) if slot <= UNITS else ("end", 0, 0)
                    if slot == 4:
                        for i in range(TILES):
                            dve.wait_ge(acc_read_act, b * ACT_READS + ACT_READS + i + 1)
                            if i:
                                wait_steps(b)
                            mark(dve.bn_stats(bn[:, i, :], v_raw[:, i, :]))
                            if i:
                                mark(dve.bn_aggr(mean_var[:, i - 1, :], bn[:, i - 1, :]))
                        wait_steps(b)
                        mark(dve.tensor_scalar(var[:, C_V:C_V + 3], mean_var[:, 0:3, 1], EPS, None, ALU.add))
                        mark(dve.bn_aggr(mean_var[:, 3, :], bn[:, 3, :]))
                        wait_steps(b)
                        step(b, dve.tensor_scalar(var[:, C_V + 3:C_V + 4], mean_var[:, 3:4, 1], EPS, None, ALU.add))
                        if not last:
                            dve.wait_ge(squares_done, b * 12 + 4 + 2)
                            mean_squares(b, C_X, C_X + 2)
                        first_guess(b, C_V, C_V + (4 if last else 6))
                    if kind == "T":
                        bank = acc[:, acc_index(slot - 1, 0) % ACC_BANKS, :]
                        reads = b * DVE_READS + 5 * a
                        what = PARTS[part]
                        dve.wait_ge(quarters, quarter(b, slot - 1)) if what != "h" else None
                        if what == "z_a":
                            dve.wait_ge(sigmoid_ready, b * 8 + 2 * a + 1)
                            dve.tensor_tensor(gate[:, 0, :], bank, gate[:, 0, :], ALU.mult).then_inc(acc_read_dve, 1)
                        if what == "u":
                            dve.wait_ge(acc_read_dve, reads + 1)
                            dve.tensor_tensor(uz[:, a, :], bank, gate[:, 0, :], ALU.mult).then_inc(acc_read_dve, 1)
                            if a == 0:
                                dve.wait_ge(rstd_ready, event(b, 0))
                            dve.tensor_scalar(v_raw[:, a, :], v_raw[:, a, :], mean_var[:, a, 0:1],
                                              rstd[:, C_V + a:C_V + a + 1], ALU.subtract, ALU.mult).then_inc(v_norm_ready, 1)
                            dve.wait_ge(v_norm_ready, b * TILES + a + 1)
                            dve.wait_ge(v_hi_ready, b * TILES + a + 1)
                            dve.tensor_tensor(x1_lo[:, a, :], v_raw[:, a, :], x1_hi[:, a, :].bitcast(F32),
                                              ALU.subtract).then_inc(v_lo_ready, 1)
                        if what == "gate_c":
                            step(b, dve.tensor_copy(xc[:, 0:2], xc_tail[:, a, :]))
                            dve.wait_ge(acc_read_act, b * ACT_READS + ACT_READS + 4 + a + 1)
                            dve.tensor_tensor(xc[:, 2:], bank, h_copy[:, :], ALU.mult).then_inc(acc_read_dve, 1)
                            dve.wait_ge(acc_read_dve, reads + 3)
                            step(b, dve.tensor_scalar(conv[:, :], xc[:, 0:HALF], conv_c[:, a, 0:1], None, ALU.mult))
                            for k in (1, 2):
                                step(b, dve.scalar_tensor_tensor(out=conv[:, :], in0=xc[:, k:k + HALF],
                                                                 scalar=conv_c[:, a, k:k + 1], in1=conv[:, :],
                                                                 op0=ALU.mult, op1=ALU.add))
                            step(b, dve.tensor_copy(xc_tail[:, a, :], xc[:, HALF:HALF + 2]))
                        if what == "gate_b":
                            dve.tensor_tensor(conv[:, :], bank, conv[:, :], ALU.mult).then_inc(acc_read_dve, 1)
                        if what == "z_b":
                            dve.wait_ge(sigmoid_ready, b * 8 + 2 * a + 2)
                            dve.tensor_tensor(gate[:, 1, :], bank, gate[:, 1, :], ALU.mult).then_inc(acc_read_dve, 1)
                            dve.wait_ge(acc_read_dve, reads + 5)
                            dve.tensor_tensor(branch[:, a % 2, :], gate[:, 1, :], conv[:, :], ALU.mult).then_inc(branch_ready, 1)
                            dve.wait_ge(branch_ready, b * 8 + a + 1)
                            dve.wait_ge(branch_hi_ready, b * 8 + a + 1)
                            dve.tensor_tensor(mix_lo[:, 4 + a, :], branch[:, a % 2, :], mix_hi[:, 4 + a, :].bitcast(F32),
                                              ALU.subtract).then_inc(branch_lo_ready, 1)
                    if kind == "O" and part == 3:
                        if a == 0:
                            dve.wait_ge(x_res_landed, b * 16 + 16)
                        for i in range(TILES):
                            dve.wait_ge(quarters, quarter(b, slot - 1, i))
                            xh = x_res[:, i, a * HALF:(a + 1) * HALF]
                            dve.tensor_tensor(xh, acc[:, acc_index(slot - 1, i) % ACC_BANKS, :], xh, ALU.add).then_inc(acc_read_dve, 1)
                    if kind == "G" and part == 3:
                        for i in range(TILES):
                            dve.wait_ge(acc_read_act, b * ACT_READS + ACT_READS + 12 + 8 * a + i + 1)
                            step(b, dve.tensor_tensor(uz[:, i, :], gate[:, i % 2, :], uz[:, i, :], ALU.mult))
                            xh = x_res[:, i, a * HALF:(a + 1) * HALF]
                            dve.tensor_tensor(xh, uz[:, i, :], xh, ALU.add).then_inc(x2_ready, 1)
                    hi_jobs = 0
                    for n, (u, (what, i, half)) in enumerate(jobs):
                        if u == slot - 1:
                            if what == "mix":
                                br = branch[:, i % 2, :]
                                dve.wait_ge(mix_done, b * heads + i + 1)
                                dve.scalar_tensor_tensor(
                                    out=br.rearrange("p (c t) -> p c t", c=TILES),
                                    in0=small[:, n % 2, :].rearrange("p (c t) -> p c t", c=TILES),
                                    scalar=ln_g_c[:, i:i + 1],
                                    in1=mix_add[:, i:i + 1, :].to_broadcast([P, TILES, P]),
                                    op0=ALU.mult, op1=ALU.add).then_inc(small_read, 1)
                                dve.wait_ge(small_read, b * JOBS + PRO_JOBS + n + 1)
                                dve.tensor_tensor(br, br, uz[:, i, :], ALU.mult).then_inc(branch_ready, 1)
                                dve.wait_ge(branch_ready, b * 8 + 4 + i + 1)
                                dve.wait_ge(branch_hi_ready, b * 8 + 4 + i + 1)
                                dve.tensor_tensor(mix_lo[:, i, :], br, mix_hi[:, i, :].bitcast(F32),
                                                  ALU.subtract).then_inc(branch_lo_ready, 1)
                            else:
                                dve.wait_ge(small_hi_ready, b * HI_JOBS + PRO_HI + hi_jobs + 1)
                                if what == "pt":
                                    small_lo(n % 2, pt_hi[:, i:i + 1, :], pt_lo[:, i:i + 1, :])
                                else:
                                    th, tl = (hn_hi, hn_lo) if what == "xt" else (x1_hi, x1_lo)
                                    small_lo(n % 2, hn_part(th, i, half), hn_part(tl, i, half))
                        if what != "mix":
                            hi_jobs += 1
                    if not last:
                        if slot in (29, 30, 38, 39):
                            i = {29: 0, 30: 1, 38: 2, 39: 3}[slot]
                            if i == 2:
                                dve.wait_ge(rstd_ready, event(b, 1))
                            normalise_x(i)
                        if slot == 34:
                            dve.wait_ge(squares_done, b * 12 + 4 + 4)
                            mean_squares(b, C_X + 2, C_X + 4)
                            first_guess(b, C_X + 2, C_X + 4)
                    if slot == 38:
                        dve.wait_ge(squares_done, b * 12 + 4 + (4 if last else 8))
                        mean_squares(b, C_X1, C_X1 + 4)
                        first_guess(b, C_X1, C_X1 + 4)
                    if slot == 47:
                        dve.wait_ge(squares_done, b * 12 + 4 + (8 if last else 12))
                        mean_squares(b, C_X2, C_X2 + 4)
                        first_guess(b, C_X2, C_X2 + 4)
                    if slot == 49:
                        dve.wait_ge(rstd_ready, event(b, 2 if last else 3))
                        for i in range(TILES):
                            dve.scalar_tensor_tensor(out=x_res[:, i, :], in0=x_res[:, i, :],
                                                     scalar=rstd[:, C_X2 + i:C_X2 + i + 1], in1=final_b[:, :],
                                                     op0=ALU.mult, op1=ALU.mult).then_inc(y_ready, 1)
                if not last:
                    assert steps[0] == VEC_BLOCK, steps[0]

            over_blocks(dve, body)


_INS = ["x", "p", "norm_g", "w_in", "ln_v_g", "ln_v_b", "w_s", "b_s", "conv_w", "w_out", "ple_norm_g",
        "w_ple_gate", "w_ple_proj", "final_g"]


def kernel(**inputs):
    import numpy as _np
    import concourse.bacc as _bacc
    from concourse import mybir as _mybir
    from concourse.bass_utils import run_bass_kernel_spmd as _run

    nc = _bacc.Bacc("TRN2", target_bir_lowering=False, num_devices=1)
    arrays, args = {}, []
    for name in _INS:
        a = _np.ascontiguousarray(inputs[name])
        arrays[f"in_{name}_dram"] = a
        args.append(nc.dram_tensor(f"in_{name}_dram", a.shape, _mybir.dt.from_np(a.dtype), kind="ExternalInput").ap())
    out = nc.dram_tensor("out_dram", inputs["x"].shape, _mybir.dt.float32, kind="ExternalOutput").ap()
    build(nc, *args, out)
    r = _run(nc, [arrays], core_ids=[0])
    return r.results[0]["out_dram"]
```

```python
from contextlib import ExitStack

import concourse.bass as bass
from concourse import mybir

P = 128
HALF = 512
F32 = mybir.dt.float32
F32R = mybir.dt.float32r
I32 = mybir.dt.int32
BF16 = mybir.dt.bfloat16
ALU = mybir.AluOpType
ACT = mybir.ActivationFunctionType
EPS = 1e-6
RSQRT_MAGIC = 0x5F3759DF
NEWTON_ROUNDS = 3

V0, T0, O0, G0, UNITS = 0, 4, 28, 36, 46
Q = 4 * UNITS
PARTS = ("z_a", "u", "h", "gate_c", "gate_b", "z_b")
O_CHUNKS = ((4, 5), (6, 7), (0, 1), (2, 3))


def unit_kind(u):
    if u < T0:
        return "V", 0, u
    if u < O0:
        return "T", (u - T0) // 6, (u - T0) % 6
    if u < G0:
        return "O", (u - O0) // 4, (u - O0) % 4
    half, part = divmod(u - G0, 5)
    return ("P", half, 0) if part == 0 else ("G", half, part - 1)


READERS = (["act"] * 4 + ["dve", "dve", "act", "dve", "dve", "dve"] * 4 + ["dve"] * 8 + ["act"] * 16)
ACC_BANKS = 6
ACT_READS = READERS.count("act")
DVE_READS = READERS.count("dve")


def acc_index(u, tile):
    kind, a, part = unit_kind(u)
    if kind == "V":
        return tile
    if kind == "T":
        return u
    if kind == "O":
        return 28 + 4 * a + tile
    return 36 + 8 * a + (4 if kind == "G" else 0) + tile


def reads_through(n):
    return READERS[:n + 1].count(READERS[n])


JOBS_AFTER = {
    27: [("mix", 0, 0), ("mix", 1, 0)],
    28: [("mix", 2, 0), ("mix", 3, 0)],
    29: [("xt", 0, 0), ("xt", 0, 1)],
    30: [("pt", 0, 0), ("pt", 1, 0)],
    31: [("xt", 1, 0), ("xt", 1, 1)],
    32: [("x1t", 0, 0), ("x1t", 1, 0)],
    33: [("x1t", 2, 0), ("x1t", 3, 0)],
    36: [("x1t", 0, 1), ("x1t", 1, 1)],
    37: [("x1t", 2, 1), ("x1t", 3, 1)],
    41: [("xt", 2, 0), ("xt", 2, 1)],
    42: [("xt", 3, 0), ("xt", 3, 1)],
}
JOBS = sum(len(v) for v in JOBS_AFTER.values())
PRO_JOBS = 10


def jobs_of(last):
    return [(u, job) for u in sorted(JOBS_AFTER) for job in JOBS_AFTER[u] if not (last and job[0] == "xt")]


def build(nc, x, p, norm_g, w_in, ln_v_g, ln_v_b, w_s, b_s, conv_w, w_out, ple_norm_g, w_ple_gate,
          w_ple_proj, final_g, out):
    _, seq, d = x.shape
    width = ln_v_g.shape[1]
    heads, chunk = b_s.shape[1], b_s.shape[2]
    ple = p.shape[3]
    KC = d // P
    TILES = HALF // P
    BLOCKS = seq // HALF
    KP = ple // P
    assert (KC, TILES, heads, chunk, width, KP) == (8, 4, 4, P, HALF, 2)
    COLUMN0 = {"u": 0, "v": width, "z_a": 2 * width, "h": 3 * width, "gate_b": 4 * width,
               "gate_c": 5 * width, "z_b": 6 * width}

    x_tiles = x[0].rearrange("(b i p) d -> b i p d", i=TILES, p=P)
    x_block = x[0].rearrange("(b i p) d -> b p i d", i=TILES, p=P)
    p_block = p[0, 0].rearrange("(b i p) c -> b p i c", i=TILES, p=P)
    out_tiles = out[0].rearrange("(b i p) d -> b i p d", i=TILES, p=P)
    w_in_k = w_in[0].rearrange("(k p) n -> p k n", p=P)
    w_out_k = w_out[0].rearrange("(k p) n -> p k n", p=P)
    w_gate_k = w_ple_gate[0].rearrange("(k p) n -> p k n", p=P)
    w_proj_k = w_ple_proj[0].rearrange("(k p) n -> p k n", p=P)

    with ExitStack() as ctx:
        def sb(name, shape, dt):
            return ctx.enter_context(nc.sbuf_tensor(name, shape, dt))

        def sem(name):
            return ctx.enter_context(nc.semaphore(name))

        hn_hi = sb("hn_hi", [P, KC, HALF], F32R)
        hn_lo = sb("hn_lo", [P, KC, HALF], F32R)
        mix_hi = sb("mix_hi", [P, KC, HALF], F32R)
        mix_lo = sb("mix_lo", [P, KC, HALF], F32R)
        x1_hi = sb("x1_hi", [P, KC, HALF], F32R)
        x1_lo = sb("x1_lo", [P, KC, HALF], F32R)
        pt_hi = sb("pt_hi", [P, KP, HALF], F32R)
        pt_lo = sb("pt_lo", [P, KP, HALF], F32R)
        wst_hi = sb("wst_hi", [P, heads, P], F32R)
        wst_lo = sb("wst_lo", [P, heads, P], F32R)
        w_hi = sb("w_hi", [P, 2, 2 * HALF], F32R)
        w_lo = sb("w_lo", [P, 2, 2 * HALF], F32R)
        ones_r = sb("ones_r", [P, P], F32R)

        w_raw = sb("w_raw", [P, 2, 2 * HALF], F32)
        x_in = sb("x_in", [P, 2, d], F32)
        x_res = sb("x_res", [P, TILES, d], F32)
        norm_b = sb("norm_b", [P, d], F32)
        final_b = sb("final_b", [P, d], F32)
        uz = sb("uz", [P, TILES, HALF], F32)
        v_raw = sb("v_raw", [P, TILES, HALF], F32)
        mix_add = sb("mix_add", [P, heads, P], F32)
        p_nat = sb("p_nat", [P, TILES, ple], F32)
        ident = sb("ident", [P, P], F32)
        xc = sb("xc", [P, HALF + 2], F32)
        xc_tail = sb("xc_tail", [P, heads, 2], F32)
        conv = sb("conv", [P, HALF], F32)
        h_copy = sb("h_copy", [P, HALF], F32)
        gate = sb("gate", [P, 2, HALF], F32)
        branch = sb("branch", [P, 2, HALF], F32)
        square = sb("square", [P, d], BF16)
        ln_g_c = sb("ln_g_c", [P, heads], F32)
        ln_b_c = sb("ln_b_c", [P, heads], F32)
        conv_c = sb("conv_c", [P, heads, 3], F32)
        ple_c = sb("ple_c", [P, KC], F32)
        bn = sb("bn", [P, TILES, 6], F32)
        mean_var = sb("mean_var", [P, TILES, 2], F32)
        sums = sb("sums", [P, 16], F32)
        var = sb("var", [P, 16], F32)
        shifted = sb("shifted", [P, 16], I32)
        rstd = sb("rstd", [P, 16], F32)
        newton = sb("newton", [P, 16], F32)
        warm = sb("warm", [P, 2], F32)
        C_V, C_X, C_X1, C_X2 = 0, 4, 8, 12

        acc = ctx.enter_context(nc.psum_tensor("acc", [P, ACC_BANKS, HALF], F32))
        small = ctx.enter_context(nc.psum_tensor("small", [P, 2, HALF], F32))

        w_landed = [sem("w_landed0"), sem("w_landed1")]
        x_first_landed = [sem(f"x_first_landed{i}") for i in range(TILES)]
        x_in_landed = [sem("x_in_landed0"), sem("x_in_landed1")]
        x_res_landed = sem("x_res_landed")
        p_landed = sem("p_landed")
        norm_landed = sem("norm_landed")
        const_landed = sem("const_landed")
        out_stored = sem("out_stored")
        quarters = sem("quarters")
        mix_done = sem("mix_done")
        xt_done = sem("xt_done")
        pt_done = sem("pt_done")
        x1t_done = sem("x1t_done")
        wst_done = sem("wst_done")
        w_hi_ready = sem("w_hi_ready")
        acc_read_act = sem("acc_read_act")
        sigmoid_ready = sem("sigmoid_ready")
        branch_hi_ready = sem("branch_hi_ready")
        v_hi_ready = sem("v_hi_ready")
        small_hi_ready = sem("small_hi_ready")
        squares_done = sem("squares_done")
        w_lo_ready = sem("w_lo_ready")
        acc_read_dve = sem("acc_read_dve")
        small_read = sem("small_read")
        v_norm_ready = sem("v_norm_ready")
        v_lo_ready = sem("v_lo_ready")
        branch_ready = sem("branch_ready")
        branch_lo_ready = sem("branch_lo_ready")
        xn_ready = sem("xn_ready")
        x2_ready = sem("x2_ready")
        y_ready = sem("y_ready")
        rstd_ready = sem("rstd_ready")
        vec_step = sem("vec_step")
        ident_ready = sem("ident_ready")
        masked = sem("masked")
        pool_set = sem("pool_set")

        VEC_PRO, VEC_BLOCK = 23, 92
        EVENTS_PRO, EVENTS = 2, 5

        block = ctx.enter_context(nc.Block())

        def w_source(u):
            kind, a, part = unit_kind(u % UNITS)
            if kind == "V":
                return w_in_k[:, 2 * part:2 * part + 2, COLUMN0["v"]:COLUMN0["v"] + HALF]
            if kind == "T":
                c = COLUMN0[PARTS[part]] + a * P
                return w_in_k[:, :, c:c + P]
            cols = slice(a * HALF, (a + 1) * HALF)
            if kind == "O":
                k = O_CHUNKS[part][0]
                return w_out_k[:, k:k + 2, cols]
            if kind == "P":
                return w_proj_k[:, :, cols]
            return w_gate_k[:, 2 * part:2 * part + 2, cols]

        def w_view(t, u):
            k = KC if unit_kind(u % UNITS)[0] == "T" else 2
            return t[:, u % 2, :].rearrange("p (k n) -> p k n", k=k)

        def quarter(b, u, tile=3):
            return b * Q + 4 * u + tile + 1

        def event(b, e):
            return b * EVENTS + EVENTS_PRO + e + 1

        def over_blocks(eng, body):
            with eng.Fori(0, BLOCKS - 1) as b:
                body(b, False)
            body(BLOCKS - 1, True)

        @block.sync
        def _(sp):
            def load_w(b, u):
                if not (isinstance(b, int) and b == 0 and u < 2):
                    sp.wait_ge(w_lo_ready, b * UNITS + u - 1)
                sp.dma_start(w_view(w_raw, u), w_source(u)).then_inc(w_landed[u % 2], 16)

            sp.sem_inc(out_stored, 16 * TILES)
            for i in range(TILES):
                sp.dma_start(x_res[:, i, :], x_tiles[0, i]).then_inc(x_first_landed[i], 16)
                if i == 1:
                    load_w(0, 0)
                    sp.dma_start(norm_b[:, :], norm_g[0:1, :].to_broadcast([P, d])).then_inc(norm_landed, 16)
            load_w(0, 1)
            sp.dma_start(uz[:, 0, :].rearrange("t (h s) -> t h s", h=heads),
                         w_s[0].rearrange("h t s -> t h s")).then_inc(const_landed, 16)
            sp.dma_start(uz[:, 1, :], b_s.rearrange("l h t -> l (h t)").to_broadcast([P, heads * P])).then_inc(const_landed, 16)
            load_w(0, 2)
            with nc.allow_non_contiguous_dma(reason="a few hundred parameters, once"):
                sp.dma_start(ln_g_c[:, :], ln_v_g[0].rearrange("(h p) -> p h", p=P)).then_inc(const_landed, 16)
                sp.dma_start(ln_b_c[:, :], ln_v_b[0].rearrange("(h p) -> p h", p=P)).then_inc(const_landed, 16)
                sp.dma_start(conv_c[:, :, :], conv_w[0].rearrange("(h p) k -> p h k", p=P)).then_inc(const_landed, 16)
                sp.dma_start(ple_c[:, :], ple_norm_g[0].rearrange("(k p) -> p k", p=P)).then_inc(const_landed, 16)
            load_w(0, 3)
            sp.dma_start(final_b[:, :], final_g.rearrange("(l n) -> l n", l=1).to_broadcast([P, d])).then_inc(const_landed, 16)
            for u in range(4, 8):
                load_w(0, u)

            def body(b, last):
                for u in range(8, UNITS if last else UNITS + 8):
                    load_w(b, u)
                    if u == 12:
                        sp.wait_ge(out_stored, (b + 1) * (16 * TILES))
                        sp.wait_ge(xt_done, b * 8 + 8)
                        sp.dma_start(x_res[:, :, :], x_block[b]).then_inc(x_res_landed, 16)
                        sp.dma_start(p_nat[:, :, :], p_block[b]).then_inc(p_landed, 16)
                    if u == 8 and not last:
                        for i in (0, 1):
                            sp.wait_ge(xt_done, b * 8 + 6 + 2 * i)
                            sp.dma_start(x_in[:, i, :], x_tiles[b + 1, i]).then_inc(x_in_landed[i], 16)
                    if u in (31, 33) and not last:
                        i = 2 if u == 31 else 3
                        sp.wait_ge(xt_done, b * 8 + 8 + 2 * (i - 1))
                        sp.dma_start(x_in[:, i % 2, :], x_tiles[b + 1, i]).then_inc(x_in_landed[i % 2], 16)
                for i in range(TILES):
                    sp.wait_ge(y_ready, b * TILES + i + 1)
                    sp.dma_start(out_tiles[b, i], x_res[:, i, :]).then_inc(out_stored, 16)

            over_blocks(sp, body)
            sp.wait_ge(out_stored, (BLOCKS + 1) * TILES * 16)

        @block.gpsimd
        def _(pool):
            pool.memset(warm[:, 0:1], 0.0).then_inc(pool_set, 1)
            pool.memset(ident[:, :], 0.0).then_inc(pool_set, 1)
            pool.memset(xc_tail[:, :, :], 0.0).then_inc(pool_set, 1)
            pool.wait_ge(pool_set, 3)
            pool.affine_select(out=ident[:, :], in_=ident[:, :], compare_op=ALU.not_equal, fill=1.0, base=0,
                               pattern=[[-1, P]], channel_multiplier=1).then_inc(ident_ready, 1)

            for u in (0, 1):
                pool.wait_ge(w_hi_ready, u + 1)
                pool.tensor_tensor(w_lo[:, u, :], w_raw[:, u, :], w_hi[:, u, :].bitcast(F32),
                                   ALU.subtract).then_inc(w_lo_ready, 1)
            pool.wait_ge(const_landed, 16 * 7)
            wsn = uz[:, 0, :].rearrange("t (h s) -> t h s", h=heads)
            pool.affine_select(out=wsn, in_=wsn, compare_op=ALU.is_ge, fill=0.0, base=0,
                               pattern=[[0, heads], [-1, P]], channel_multiplier=1).then_inc(masked, 1)

        @block.tensor
        def _(pe):
            def product(ps, left_hi, left_lo, right_hi, right_lo, first, last):
                pe.matmul(ps, left_hi, right_hi, start=first, stop=False)
                pe.matmul(ps, left_hi, right_lo, start=False, stop=False)
                return pe.matmul(ps, left_lo, right_hi, start=False, stop=last)

            def wait_bank(b, n):
                if n >= ACC_BANKS:
                    m = n - ACC_BANKS
                    if READERS[m] == "act":
                        pe.wait_ge(acc_read_act, b * ACT_READS + ACT_READS + reads_through(m))
                    else:
                        pe.wait_ge(acc_read_dve, b * DVE_READS + reads_through(m))
                else:
                    m = max(i for i in range(len(READERS)) if i % ACC_BANKS == n)
                    pe.wait_ge(acc_read_act, b * ACT_READS + reads_through(m))

            def unit(b, u, tiles=range(TILES)):
                kind, a, part = unit_kind(u)
                pe.wait_ge(w_lo_ready, b * UNITS + u + 1)
                hi, lo = w_view(w_hi, u), w_view(w_lo, u)
                if kind == "T":
                    n = acc_index(u, 0)
                    wait_bank(b, n)
                    for k in range(KC):
                        ins = product(acc[:, n % ACC_BANKS, :], hi[:, k, :], lo[:, k, :],
                                      hn_hi[:, k, :], hn_lo[:, k, :], k == 0, k == KC - 1)
                        if k % 2:
                            ins.then_inc(quarters, 1)
                    return
                left_hi, left_lo, k0, first, last = {
                    "V": (hn_hi, hn_lo, 2 * part, part == 0, part == 3),
                    "O": (mix_hi, mix_lo, O_CHUNKS[part][0], part == 0, part == 3),
                    "P": (pt_hi, pt_lo, 0, True, True),
                    "G": (x1_hi, x1_lo, 2 * part, part == 0, part == 3),
                }[kind]
                for i in tiles:
                    n = acc_index(u, i)
                    if first:
                        wait_bank(b, n)
                    for kk in range(2):
                        k, t = k0 + kk, slice(i * P, (i + 1) * P)
                        ins = product(acc[:, n % ACC_BANKS, :], left_hi[:, k, t], left_lo[:, k, t],
                                      hi[:, kk, :], lo[:, kk, :], first and kk == 0, last and kk == 1)
                    ins.then_inc(quarters, 1)

            def transposes(bank, sources, done):
                for n, s in enumerate(sources):
                    ins = pe.transpose(small[:, bank, n * P:(n + 1) * P], s, ident[:, :])
                ins.then_inc(done, 1)

            def first_xt(i):
                pe.wait_ge(xn_ready, i + 1)
                for half in range(2):
                    if i:
                        pe.wait_ge(small_read, 2 * i + half - 1)
                    transposes(half, [x_res[:, i, (4 * half + k) * P:(4 * half + k + 1) * P] for k in range(4)], xt_done)

            def first_v(i):
                pe.wait_ge(small_read, 2 * i + 2)
                unit(0, 0, (i,))

            pe.wait_ge(ident_ready, 1)
            first_xt(0)
            first_xt(1)
            first_v(0)
            first_xt(2)
            first_v(1)
            first_xt(3)
            first_v(2)
            first_v(3)
            pe.wait_ge(masked, 1)
            transposes(0, [uz[:, 0, h * P:(h + 1) * P] for h in range(heads)], wst_done)
            pe.wait_ge(small_read, 9)
            pe.matmul(small[:, 1, :], ones_r[:, :], wst_hi[:, :, :], start=True, stop=False)
            pe.matmul(small[:, 1, :], ones_r[:, :], wst_lo[:, :, :], start=False, stop=True).then_inc(wst_done, 1)

            def body(b, last):
                index = {job: n for n, (_, job) in enumerate(jobs_of(last))}

                def small_count(job):
                    return b * JOBS + PRO_JOBS + index[job] + 1

                for u in range(1, UNITS if last else UNITS + 1):
                    if u == UNITS:
                        pe.wait_ge(small_read, b * JOBS + PRO_JOBS + JOBS)
                        unit(b + 1, 0)
                        continue
                    kind, a, part = unit_kind(u)
                    if kind == "O" and a == 0:
                        pe.wait_ge(branch_lo_ready, b * 8 + 2 * (part + 1))
                    if kind == "P" and a == 0:
                        pe.wait_ge(small_read, small_count(("pt", 1, 0)))
                    if kind == "G" and a == 0 and part in (0, 2):
                        pe.wait_ge(small_read, small_count(("x1t", 3, part // 2)))
                    unit(b, u)
                    for job in JOBS_AFTER.get(u, ()):
                        if job not in index:
                            continue
                        what, i, half = job
                        n = index[job]
                        pe.wait_ge(small_read, b * JOBS + PRO_JOBS + n - 1)
                        if what == "mix":
                            pe.wait_ge(v_lo_ready, b * TILES + TILES)
                            for c in range(TILES):
                                hs = slice(i * P, (i + 1) * P)
                                ins = product(small[:, n % 2, c * P:(c + 1) * P], x1_hi[:, c, hs], x1_lo[:, c, hs],
                                              wst_hi[:, i, :], wst_lo[:, i, :], True, True)
                            ins.then_inc(mix_done, 1)
                        elif what == "xt":
                            pe.wait_ge(xn_ready, b * TILES + TILES + i + 1)
                            xt_bank = n % 2
                            transposes(xt_bank, [x_in[:, i % 2, (4 * half + k) * P:(4 * half + k + 1) * P]
                                                 for k in range(4)], xt_done)
                        elif what == "pt":
                            pe.wait_ge(p_landed, b * 16 + 16)
                            transposes(n % 2, [p_nat[:, t, i * P:(i + 1) * P] for t in range(TILES)], pt_done)
                        else:
                            pe.wait_ge(acc_read_dve, b * DVE_READS + reads_through(28 + 4 * half + i))
                            transposes(n % 2, [x_res[:, i, (4 * half + k) * P:(4 * half + k + 1) * P]
                                               for k in range(4)], x1t_done)

            over_blocks(pe, body)

        @block.scalar
        def _(act):
            act.sem_inc(acc_read_act, ACT_READS)

            def sigmoid_table():
                act.activation(warm[:, 1:2], warm[:, 0:1], ACT.Sigmoid)

            def split_hi(b, u):
                act.wait_ge(w_landed[u % 2], (b * (UNITS // 2) + u // 2 + 1) * 16)
                if not (isinstance(b, int) and b == 0 and u < 2):
                    act.wait_ge(quarters, b * Q + 4 * (u - 1))
                if unit_kind(u % UNITS)[0] == "G":
                    k = 2 * unit_kind(u)[2]
                    for kk in range(2):
                        ins = act.activation(w_view(w_hi, u)[:, kk, :], w_view(w_raw, u)[:, kk, :], ACT.Copy,
                                             scale=ple_c[:, k + kk:k + kk + 1])
                else:
                    ins = act.activation(w_hi[:, u % 2, :], w_raw[:, u % 2, :], ACT.Copy)
                ins.then_inc(w_hi_ready, 1)

            def squares(source, col, done):
                if done is not None:
                    act.wait_ge(squares_done, done)
                act.activation(square[:, :], source, ACT.Square, accum_out=sums[:, col:col + 1]).then_inc(squares_done, 1)

            def small_hi(bank, target):
                k = target.shape[1]
                act.activation(target, small[:, bank, :].rearrange("p (k n) -> p k n", k=k),
                               ACT.Copy).then_inc(small_hi_ready, 1)

            def hn_part(t, i, half):
                return t[:, 4 * half:4 * half + 4, i * P:(i + 1) * P]

            act.wait_ge(pool_set, 1)
            sigmoid_table()
            for i in range(TILES):
                act.wait_ge(x_first_landed[i], 16)
                squares(x_res[:, i, :], C_X + i, i or None)
                if i % 2:
                    split_hi(0, i // 2)
            for i in range(TILES):
                for half in range(2):
                    act.wait_ge(xt_done, 2 * i + half + 1)
                    small_hi(half, hn_part(hn_hi, i, half))
            act.wait_ge(wst_done, 1)
            small_hi(0, wst_hi[:, :, :])
            for u in range(2, 5):
                split_hi(0, u)

            PRO_HI, HI_JOBS = 9, JOBS - heads

            def body(b, last):
                jobs = jobs_of(last)
                sigmoid_table()
                for slot in range(4, 50):
                    if not last or slot + 1 < UNITS:
                        split_hi(b, slot + 1)
                    kind, a, part = unit_kind(slot - 1) if slot <= UNITS else ("end", 0, 0)
                    if slot == 4:
                        for i in range(TILES):
                            act.wait_ge(quarters, quarter(b, 3, i))
                            act.activation(v_raw[:, i, :], acc[:, acc_index(3, i) % ACC_BANKS, :], ACT.Copy).then_inc(acc_read_act, 1)
                    if kind == "T":
                        bank = acc[:, acc_index(slot - 1, 0) % ACC_BANKS, :]
                        what = PARTS[part]
                        if what in ("z_a", "z_b"):
                            g = 0 if what == "z_a" else 1
                            act.wait_ge(quarters, quarter(b, slot - 1))
                            if a:
                                if g == 0:
                                    act.wait_ge(acc_read_dve, b * DVE_READS + 5 * (a - 1) + 2)
                                else:
                                    act.wait_ge(branch_ready, b * 8 + a)
                            act.activation(gate[:, g, :], bank, ACT.Sigmoid).then_inc(sigmoid_ready, 1)
                        if what == "u":
                            act.wait_ge(v_norm_ready, b * TILES + a + 1)
                            act.activation(x1_hi[:, a, :], v_raw[:, a, :], ACT.Copy).then_inc(v_hi_ready, 1)
                        if what == "h":
                            act.wait_ge(quarters, quarter(b, slot - 1))
                            if a:
                                act.wait_ge(acc_read_dve, b * DVE_READS + 5 * (a - 1) + 3)
                            act.activation(h_copy[:, :], bank, ACT.Copy).then_inc(acc_read_act, 1)
                        if what == "z_b":
                            act.wait_ge(branch_ready, b * 8 + a + 1)
                            act.activation(mix_hi[:, 4 + a, :], branch[:, a % 2, :], ACT.Copy).then_inc(branch_hi_ready, 1)
                    if kind == "P":
                        for i in range(TILES):
                            act.wait_ge(quarters, quarter(b, slot - 1, i))
                            act.activation((uz, v_raw)[a][:, i, :], acc[:, acc_index(slot - 1, i) % ACC_BANKS, :],
                                           ACT.Copy).then_inc(acc_read_act, 1)
                    if kind == "G" and part == 3:
                        if a == 0:
                            act.wait_ge(rstd_ready, event(b, 1 if last else 2))
                        for i in range(TILES):
                            act.wait_ge(quarters, quarter(b, slot - 1, i))
                            if 4 * a + i >= 2:
                                act.wait_ge(x2_ready, b * 8 + 4 * a + i - 1)
                            act.activation(gate[:, i % 2, :], acc[:, acc_index(slot - 1, i) % ACC_BANKS, :],
                                           ACT.Sigmoid, scale=rstd[:, C_X1 + i:C_X1 + i + 1]).then_inc(acc_read_act, 1)
                    for n, (u, (what, i, half)) in enumerate(jobs):
                        if u != slot - 1:
                            continue
                        if what == "mix":
                            act.wait_ge(branch_ready, b * 8 + 4 + i + 1)
                            act.activation(mix_hi[:, i, :], branch[:, i % 2, :], ACT.Copy).then_inc(branch_hi_ready, 1)
                        elif what == "xt":
                            act.wait_ge(xt_done, b * 8 + 8 + 2 * i + half + 1)
                            small_hi(n % 2, hn_part(hn_hi, i, half))
                        elif what == "pt":
                            act.wait_ge(pt_done, b * KP + i + 1)
                            small_hi(n % 2, pt_hi[:, i:i + 1, :])
                        else:
                            act.wait_ge(x1t_done, b * 8 + 4 * half + i + 1)
                            small_hi(n % 2, hn_part(x1_hi, i, half))
                    if slot == 10 and not last:
                        for i in (0, 1):
                            act.wait_ge(x_in_landed[i], (b * 2 + 1) * 16)
                            squares(x_in[:, i, :], C_X + i, b * 12 + 4 + i)
                    if slot == 34 and not last:
                        for i in (2, 3):
                            act.wait_ge(x_in_landed[i % 2], (b * 2 + 2) * 16)
                            squares(x_in[:, i % 2, :], C_X + i, b * 12 + 4 + i)
                    if slot == 37:
                        for i in range(TILES):
                            act.wait_ge(acc_read_dve, b * DVE_READS + 25 + i)
                            squares(x_res[:, i, :], C_X1 + i, b * 12 + 4 + (0 if last else 4) + i)
                    if slot == 47:
                        for i in range(TILES):
                            act.wait_ge(x2_ready, b * 8 + 4 + i + 1)
                            squares(x_res[:, i, :], C_X2 + i, b * 12 + 4 + (4 if last else 8) + i)

            over_blocks(act, body)

        @block.vector
        def _(dve):
            steps = [0]

            def mark(ins):
                steps[0] += 1
                ins.then_inc(vec_step, 1)

            def step(b, ins):
                mark(ins)
                wait_steps(b)

            def wait_steps(b):
                if b is None:
                    dve.wait_ge(vec_step, steps[0])
                else:
                    dve.wait_ge(vec_step, b * VEC_BLOCK + VEC_PRO + steps[0])

            def split_lo(b, u):
                dve.wait_ge(w_hi_ready, b * UNITS + u + 1)
                if unit_kind(u % UNITS)[0] == "G":
                    k = 2 * unit_kind(u)[2]
                    for kk in range(2):
                        ins = dve.scalar_tensor_tensor(
                            out=w_view(w_lo, u)[:, kk, :], in0=w_view(w_raw, u)[:, kk, :],
                            scalar=ple_c[:, k + kk:k + kk + 1], in1=w_view(w_hi, u)[:, kk, :].bitcast(F32),
                            op0=ALU.mult, op1=ALU.subtract)
                else:
                    ins = dve.tensor_tensor(w_lo[:, u % 2, :], w_raw[:, u % 2, :],
                                            w_hi[:, u % 2, :].bitcast(F32), ALU.subtract)
                ins.then_inc(w_lo_ready, 1)

            def small_lo(bank, hi, lo):
                k = lo.shape[1]
                dve.tensor_tensor(lo, small[:, bank, :].rearrange("p (k n) -> p k n", k=k),
                                  hi.bitcast(F32), ALU.subtract).then_inc(small_read, 1)

            def hn_part(t, i, half):
                return t[:, 4 * half:4 * half + 4, i * P:(i + 1) * P]

            def mean_squares(b, c0, c1):
                step(b, dve.tensor_scalar(var[:, c0:c1], sums[:, c0:c1], 1.0 / d, EPS, ALU.mult, ALU.add))

            def rsqrt(b, c0, c1):
                y, v, t = (m[:, c0:c1] for m in (rstd, var, newton))
                step(b, dve.tensor_scalar(shifted[:, c0:c1], v.bitcast(I32), 1, None, ALU.logical_shift_right))
                step(b, dve.tensor_scalar(y.bitcast(I32), shifted[:, c0:c1], -1.0, float(RSQRT_MAGIC),
                                          ALU.mult, ALU.add))
                for r in range(NEWTON_ROUNDS):
                    step(b, dve.scalar_tensor_tensor(out=t, in0=y, scalar=-0.5, in1=y, op0=ALU.mult, op1=ALU.mult))
                    step(b, dve.tensor_tensor(t, t, v, ALU.mult))
                    ins = dve.scalar_tensor_tensor(out=y, in0=t, scalar=1.5, in1=y, op0=ALU.add, op1=ALU.mult)
                    if r < NEWTON_ROUNDS - 1:
                        step(b, ins)
                ins.then_inc(rstd_ready, 1)

            def normalise_x(tile, i):
                dve.scalar_tensor_tensor(out=tile, in0=tile, scalar=rstd[:, C_X + i:C_X + i + 1], in1=norm_b[:, :],
                                         op0=ALU.mult, op1=ALU.mult).then_inc(xn_ready, 1)

            def first_lo(i):
                for half in range(2):
                    dve.wait_ge(small_hi_ready, 2 * i + half + 1)
                    small_lo(half, hn_part(hn_hi, i, half), hn_part(hn_lo, i, half))

            step(None, dve.memset(ones_r[:, :].bitcast(F32), 1.0))
            for pair in range(2):
                c0 = C_X + 2 * pair
                dve.wait_ge(squares_done, 2 * pair + 2)
                mean_squares(None, c0, c0 + 2)
                rsqrt(None, c0, c0 + 2)
                if pair == 0:
                    dve.wait_ge(norm_landed, 16)
                dve.wait_ge(rstd_ready, pair + 1)
                normalise_x(x_res[:, 2 * pair, :], 2 * pair)
                normalise_x(x_res[:, 2 * pair + 1, :], 2 * pair + 1)
                first_lo(2 * pair)
                if pair:
                    first_lo(3)
                else:
                    first_lo(1)
            dve.wait_ge(w_lo_ready, 2)
            dve.wait_ge(small_hi_ready, 9)
            small_lo(0, wst_hi[:, :, :], wst_lo[:, :, :])
            for u in range(2, 5):
                split_lo(0, u)
                if u == 2:
                    dve.wait_ge(wst_done, 2)
                    dve.wait_ge(const_landed, 16 * 7)
                    for h in range(heads):
                        ins = dve.scalar_tensor_tensor(
                            out=mix_add[:, h, :], in0=small[:, 1, h * P:(h + 1) * P], scalar=ln_b_c[:, h:h + 1],
                            in1=uz[:, 1, h * P:(h + 1) * P], op0=ALU.mult, op1=ALU.add)
                    ins.then_inc(small_read, 1)
            assert steps[0] == VEC_PRO

            PRO_HI, HI_JOBS = 9, JOBS - heads

            def body(b, last):
                steps[0] = 0
                jobs = jobs_of(last)
                for slot in range(4, 50):
                    if not last or slot + 1 < UNITS:
                        split_lo(b, slot + 1)
                    kind, a, part = unit_kind(slot - 1) if slot <= UNITS else ("end", 0, 0)
                    if slot == 4:
                        for i in range(TILES):
                            dve.wait_ge(acc_read_act, b * ACT_READS + ACT_READS + i + 1)
                            if i:
                                wait_steps(b)
                            mark(dve.bn_stats(bn[:, i, :], v_raw[:, i, :]))
                            if i:
                                mark(dve.bn_aggr(mean_var[:, i - 1, :], bn[:, i - 1, :]))
                        wait_steps(b)
                        mark(dve.tensor_scalar(var[:, C_V:C_V + 3], mean_var[:, 0:3, 1], EPS, None, ALU.add))
                        mark(dve.bn_aggr(mean_var[:, 3, :], bn[:, 3, :]))
                        wait_steps(b)
                        step(b, dve.tensor_scalar(var[:, C_V + 3:C_V + 4], mean_var[:, 3:4, 1], EPS, None, ALU.add))
                        rsqrt(b, C_V, C_V + 4)
                    if kind == "T":
                        bank = acc[:, acc_index(slot - 1, 0) % ACC_BANKS, :]
                        reads = b * DVE_READS + 5 * a
                        what = PARTS[part]
                        dve.wait_ge(quarters, quarter(b, slot - 1)) if what != "h" else None
                        if what == "z_a":
                            dve.wait_ge(sigmoid_ready, b * 8 + 2 * a + 1)
                            dve.tensor_tensor(gate[:, 0, :], bank, gate[:, 0, :], ALU.mult).then_inc(acc_read_dve, 1)
                        if what == "u":
                            dve.wait_ge(acc_read_dve, reads + 1)
                            dve.tensor_tensor(uz[:, a, :], bank, gate[:, 0, :], ALU.mult).then_inc(acc_read_dve, 1)
                            if a == 0:
                                dve.wait_ge(rstd_ready, event(b, 0))
                            dve.tensor_scalar(v_raw[:, a, :], v_raw[:, a, :], mean_var[:, a, 0:1],
                                              rstd[:, C_V + a:C_V + a + 1], ALU.subtract, ALU.mult).then_inc(v_norm_ready, 1)
                            dve.wait_ge(v_norm_ready, b * TILES + a + 1)
                            dve.wait_ge(v_hi_ready, b * TILES + a + 1)
                            dve.tensor_tensor(x1_lo[:, a, :], v_raw[:, a, :], x1_hi[:, a, :].bitcast(F32),
                                              ALU.subtract).then_inc(v_lo_ready, 1)
                        if what == "gate_c":
                            step(b, dve.tensor_copy(xc[:, 0:2], xc_tail[:, a, :]))
                            dve.wait_ge(acc_read_act, b * ACT_READS + ACT_READS + 4 + a + 1)
                            dve.tensor_tensor(xc[:, 2:], bank, h_copy[:, :], ALU.mult).then_inc(acc_read_dve, 1)
                            dve.wait_ge(acc_read_dve, reads + 3)
                            step(b, dve.tensor_scalar(conv[:, :], xc[:, 0:HALF], conv_c[:, a, 0:1], None, ALU.mult))
                            for k in (1, 2):
                                step(b, dve.scalar_tensor_tensor(out=conv[:, :], in0=xc[:, k:k + HALF],
                                                                 scalar=conv_c[:, a, k:k + 1], in1=conv[:, :],
                                                                 op0=ALU.mult, op1=ALU.add))
                            step(b, dve.tensor_copy(xc_tail[:, a, :], xc[:, HALF:HALF + 2]))
                        if what == "gate_b":
                            dve.tensor_tensor(conv[:, :], bank, conv[:, :], ALU.mult).then_inc(acc_read_dve, 1)
                        if what == "z_b":
                            dve.wait_ge(sigmoid_ready, b * 8 + 2 * a + 2)
                            dve.tensor_tensor(gate[:, 1, :], bank, gate[:, 1, :], ALU.mult).then_inc(acc_read_dve, 1)
                            dve.wait_ge(acc_read_dve, reads + 5)
                            dve.tensor_tensor(branch[:, a % 2, :], gate[:, 1, :], conv[:, :], ALU.mult).then_inc(branch_ready, 1)
                            dve.wait_ge(branch_ready, b * 8 + a + 1)
                            dve.wait_ge(branch_hi_ready, b * 8 + a + 1)
                            dve.tensor_tensor(mix_lo[:, 4 + a, :], branch[:, a % 2, :], mix_hi[:, 4 + a, :].bitcast(F32),
                                              ALU.subtract).then_inc(branch_lo_ready, 1)
                    if kind == "O" and part == 3:
                        if a == 0:
                            dve.wait_ge(x_res_landed, b * 16 + 16)
                        for i in range(TILES):
                            dve.wait_ge(quarters, quarter(b, slot - 1, i))
                            xh = x_res[:, i, a * HALF:(a + 1) * HALF]
                            dve.tensor_tensor(xh, acc[:, acc_index(slot - 1, i) % ACC_BANKS, :], xh, ALU.add).then_inc(acc_read_dve, 1)
                    if kind == "G" and part == 3:
                        for i in range(TILES):
                            dve.wait_ge(acc_read_act, b * ACT_READS + ACT_READS + 12 + 8 * a + i + 1)
                            pp = (uz, v_raw)[a][:, i, :]
                            step(b, dve.tensor_tensor(pp, gate[:, i % 2, :], pp, ALU.mult))
                            xh = x_res[:, i, a * HALF:(a + 1) * HALF]
                            dve.tensor_tensor(xh, pp, xh, ALU.add).then_inc(x2_ready, 1)
                    hi_jobs = 0
                    for n, (u, (what, i, half)) in enumerate(jobs):
                        if u == slot - 1:
                            if what == "mix":
                                br = branch[:, i % 2, :]
                                dve.wait_ge(mix_done, b * heads + i + 1)
                                dve.scalar_tensor_tensor(
                                    out=br.rearrange("p (c t) -> p c t", c=TILES),
                                    in0=small[:, n % 2, :].rearrange("p (c t) -> p c t", c=TILES),
                                    scalar=ln_g_c[:, i:i + 1],
                                    in1=mix_add[:, i:i + 1, :].to_broadcast([P, TILES, P]),
                                    op0=ALU.mult, op1=ALU.add).then_inc(small_read, 1)
                                dve.wait_ge(small_read, b * JOBS + PRO_JOBS + n + 1)
                                dve.tensor_tensor(br, br, uz[:, i, :], ALU.mult).then_inc(branch_ready, 1)
                                dve.wait_ge(branch_ready, b * 8 + 4 + i + 1)
                                dve.wait_ge(branch_hi_ready, b * 8 + 4 + i + 1)
                                dve.tensor_tensor(mix_lo[:, i, :], br, mix_hi[:, i, :].bitcast(F32),
                                                  ALU.subtract).then_inc(branch_lo_ready, 1)
                            else:
                                dve.wait_ge(small_hi_ready, b * HI_JOBS + PRO_HI + hi_jobs + 1)
                                if what == "pt":
                                    small_lo(n % 2, pt_hi[:, i:i + 1, :], pt_lo[:, i:i + 1, :])
                                else:
                                    th, tl = (hn_hi, hn_lo) if what == "xt" else (x1_hi, x1_lo)
                                    small_lo(n % 2, hn_part(th, i, half), hn_part(tl, i, half))
                        if what != "mix":
                            hi_jobs += 1
                    if not last:
                        if slot in (11, 39):
                            c0 = C_X if slot == 11 else C_X + 2
                            dve.wait_ge(squares_done, b * 12 + 4 + (2 if slot == 11 else 4))
                            mean_squares(b, c0, c0 + 2)
                            rsqrt(b, c0, c0 + 2)
                        for i in {17: (0,), 23: (1,), 40: (2, 3)}.get(slot, ()):
                            if i in (0, 2):
                                dve.wait_ge(rstd_ready, event(b, 1 + i))
                            normalise_x(x_in[:, i % 2, :], i)
                    if slot == 38:
                        dve.wait_ge(squares_done, b * 12 + 4 + (4 if last else 8))
                        mean_squares(b, C_X1, C_X1 + 4)
                        rsqrt(b, C_X1, C_X1 + 4)
                    if slot == 47:
                        dve.wait_ge(squares_done, b * 12 + 4 + (8 if last else 12))
                        mean_squares(b, C_X2, C_X2 + 4)
                        rsqrt(b, C_X2, C_X2 + 4)
                    if slot == 49:
                        dve.wait_ge(rstd_ready, event(b, 2 if last else 4))
                        for i in range(TILES):
                            dve.scalar_tensor_tensor(out=x_res[:, i, :], in0=x_res[:, i, :],
                                                     scalar=rstd[:, C_X2 + i:C_X2 + i + 1], in1=final_b[:, :],
                                                     op0=ALU.mult, op1=ALU.mult).then_inc(y_ready, 1)
                if not last:
                    assert steps[0] == VEC_BLOCK, steps[0]

            over_blocks(dve, body)


_INS = ["x", "p", "norm_g", "w_in", "ln_v_g", "ln_v_b", "w_s", "b_s", "conv_w", "w_out", "ple_norm_g",
        "w_ple_gate", "w_ple_proj", "final_g"]


def kernel(**inputs):
    import numpy as _np
    import concourse.bacc as _bacc
    from concourse import mybir as _mybir
    from concourse.bass_utils import run_bass_kernel_spmd as _run

    nc = _bacc.Bacc("TRN2", target_bir_lowering=False, num_devices=1)
    arrays, args = {}, []
    for name in _INS:
        a = _np.ascontiguousarray(inputs[name])
        arrays[f"in_{name}_dram"] = a
        args.append(nc.dram_tensor(f"in_{name}_dram", a.shape, _mybir.dt.from_np(a.dtype), kind="ExternalInput").ap())
    out = nc.dram_tensor("out_dram", inputs["x"].shape, _mybir.dt.float32, kind="ExternalOutput").ap()
    build(nc, *args, out)
    r = _run(nc, [arrays], core_ids=[0])
    return r.results[0]["out_dram"]
```

```python
from contextlib import ExitStack

import concourse.bass as bass
from concourse import mybir

P = 128
HALF = 512
F32 = mybir.dt.float32
F32R = mybir.dt.float32r
I32 = mybir.dt.int32
BF16 = mybir.dt.bfloat16
ALU = mybir.AluOpType
ACT = mybir.ActivationFunctionType
EPS = 1e-6
RSQRT_MAGIC = 0x5F3759DF
NEWTON_ROUNDS = 3

V0, T0, O0, G0, UNITS = 0, 4, 28, 36, 46
TILES_A_BLOCK = 4
Q = TILES_A_BLOCK * UNITS
PARTS = ("z_a", "u", "h", "gate_c", "gate_b", "z_b")
MIX_ORDER = (4, 0, 5, 1, 2, 6, 3, 7)
O_CHUNKS = ((0, 1), (4, 5), (2, 3), (6, 7))


def unit_kind(u):
    if u < T0:
        return "V", 0, u
    if u < O0:
        return "T", (u - T0) // 6, (u - T0) % 6
    if u < G0:
        return "O", (u - O0) // 4, (u - O0) % 4
    half, part = divmod(u - G0, 5)
    return ("P", half, 0) if part == 0 else ("G", half, part - 1)


READERS = (["act"] * 4 + ["dve", "dve", "act", "dve", "dve", "dve"] * 4 + ["dve"] * 8 + ["act"] * 16)
ACC_BANKS = 6
ACT_READS = READERS.count("act")
DVE_READS = READERS.count("dve")


def acc_index(u, tile):
    kind, a, part = unit_kind(u)
    if kind == "V":
        return tile
    if kind == "T":
        return u
    if kind == "O":
        return 28 + 4 * a + tile
    return 36 + 8 * a + (4 if kind == "G" else 0) + tile


def bank_of(n):
    return (n if n < 8 else n + 2) % ACC_BANKS


def unit_of(n):
    return max(u for u in range(UNITS) if acc_index(u, 0) <= n <= acc_index(u, TILES_A_BLOCK - 1))


def reads_through(n):
    return READERS[:n + 1].count(READERS[n])


READ_FIRST = (32, 36, 46)

JOBS_AFTER = {
    14: [("mix", 0, 0)],
    18: [("mix", 1, 0)],
    20: [("mix", 2, 0)],
    26: [("mix", 3, 0)],
    29: [("xt", 0, 0), ("xt", 0, 1)],
    30: [("pt", 0, 0), ("pt", 1, 0)],
    31: [("xt", 1, 0), ("xt", 1, 1)],
    32: [("x1t", 0, 0), ("x1t", 1, 0)],
    33: [("x1t", 2, 0), ("x1t", 3, 0)],
    36: [("x1t", 0, 1), ("x1t", 1, 1)],
    37: [("x1t", 2, 1), ("x1t", 3, 1)],
    41: [("xt", 2, 0), ("xt", 2, 1)],
    42: [("xt", 3, 0), ("xt", 3, 1)],
}
JOBS = sum(len(v) for v in JOBS_AFTER.values())
PRO_JOBS = 10


def made(k):
    return MIX_ORDER.index(k) + 1


def v_tile(head, what):
    return {("u", 0): 0, ("h", 0): 1, ("u", 1): 2, ("h", 1): 3}.get((what, head))


def jobs_of(last):
    return [(u, job) for u in sorted(JOBS_AFTER) for job in JOBS_AFTER[u] if not (last and job[0] == "xt")]


def build(nc: bass.Bass, x, p, norm_g, w_in, ln_v_g, ln_v_b, w_s, b_s, conv_w, w_out, ple_norm_g, w_ple_gate,
          w_ple_proj, final_g, out):
    _, seq, d = x.shape
    width = ln_v_g.shape[1]
    heads, chunk = b_s.shape[1], b_s.shape[2]
    ple = p.shape[3]
    KC = d // P
    TILES = HALF // P
    BLOCKS = seq // HALF
    KP = ple // P
    assert (KC, TILES, heads, chunk, width, KP) == (8, 4, 4, P, HALF, 2)
    COLUMN0 = {"u": 0, "v": width, "z_a": 2 * width, "h": 3 * width, "gate_b": 4 * width,
               "gate_c": 5 * width, "z_b": 6 * width}

    x_tiles = x[0].rearrange("(b i p) d -> b i p d", i=TILES, p=P)
    x_block = x[0].rearrange("(b i p) d -> b p i d", i=TILES, p=P)
    p_block = p[0, 0].rearrange("(b i p) c -> b p i c", i=TILES, p=P)
    out_tiles = out[0].rearrange("(b i p) d -> b i p d", i=TILES, p=P)
    w_in_k = w_in[0].rearrange("(k p) n -> p k n", p=P)
    w_out_k = w_out[0].rearrange("(k p) n -> p k n", p=P)
    w_gate_k = w_ple_gate[0].rearrange("(k p) n -> p k n", p=P)
    w_proj_k = w_ple_proj[0].rearrange("(k p) n -> p k n", p=P)

    with ExitStack() as ctx:
        def sb(name, shape, dt):
            return ctx.enter_context(nc.sbuf_tensor(name, shape, dt))

        def sem(name):
            return ctx.enter_context(nc.semaphore(name))

        hn_hi = sb("hn_hi", [P, KC, HALF], F32R)
        hn_lo = sb("hn_lo", [P, KC, HALF], F32R)
        mix_hi = sb("mix_hi", [P, KC, HALF], F32R)
        mix_lo = sb("mix_lo", [P, KC, HALF], F32R)
        x1_hi = sb("x1_hi", [P, KC, HALF], F32R)
        x1_lo = sb("x1_lo", [P, KC, HALF], F32R)
        pt_hi = sb("pt_hi", [P, KP, HALF], F32R)
        pt_lo = sb("pt_lo", [P, KP, HALF], F32R)
        wst = sb("wst", [P, heads, 2, P], F32R)
        wst_hi, wst_lo = wst[:, :, 0, :], wst[:, :, 1, :]
        w_hi = sb("w_hi", [P, 2, 2 * HALF], F32R)
        w_lo = sb("w_lo", [P, 2, 2 * HALF], F32R)
        ones_r = sb("ones_r", [P, P], F32R)

        w_raw = sb("w_raw", [P, 2, 2 * HALF], F32)
        x_in = sb("x_in", [P, 2, d], F32)
        x_res = sb("x_res", [P, TILES, d], F32)
        norm_b = sb("norm_b", [P, d], F32)
        final_b = sb("final_b", [P, d], F32)
        uz = sb("uz", [P, TILES, HALF], F32)
        v_raw = sb("v_raw", [P, TILES, HALF], F32)
        mix_add = sb("mix_add", [P, heads, P], F32)
        p_nat = sb("p_nat", [P, TILES, ple], F32)
        ident = sb("ident", [P, P], F32)
        xc = sb("xc", [P, HALF + 2], F32)
        xc_tail = sb("xc_tail", [P, heads, 2], F32)
        conv = sb("conv", [P, HALF], F32)
        h_copy = sb("h_copy", [P, HALF], F32)
        gate = sb("gate", [P, 2, HALF], F32)
        branch = sb("branch", [P, 2, HALF], F32)
        square = sb("square", [P, d], BF16)
        ln_g_c = sb("ln_g_c", [P, heads], F32)
        ln_b_c = sb("ln_b_c", [P, heads], F32)
        conv_c = sb("conv_c", [P, heads, 3], F32)
        ple_c = sb("ple_c", [P, KC], F32)
        bn = sb("bn", [P, TILES, 6], F32)
        mean_var = sb("mean_var", [P, TILES, 2], F32)
        sums = sb("sums", [P, 16], F32)
        var = sb("var", [P, 16], F32)
        shifted = sb("shifted", [P, 16], I32)
        rstd = sb("rstd", [P, 16], F32)
        newton = sb("newton", [P, 16], F32)
        warm = sb("warm", [P, 2], F32)
        C_V, C_X, C_X1, C_X2 = 0, 4, 8, 12

        acc = ctx.enter_context(nc.psum_tensor("acc", [P, ACC_BANKS, HALF], F32))
        small = ctx.enter_context(nc.psum_tensor("small", [P, 2, HALF], F32))
        mixed = small[:, :, :].rearrange("p b (c h t) -> p (b c) h t", h=2, t=P)

        w_landed = [sem("w_landed0"), sem("w_landed1")]
        x_first_landed = [sem(f"x_first_landed{i}") for i in range(TILES)]
        x_in_landed = [sem("x_in_landed0"), sem("x_in_landed1")]
        x_res_landed = sem("x_res_landed")
        p_landed = sem("p_landed")
        norm_landed = sem("norm_landed")
        const_landed = sem("const_landed")
        w_s_landed = sem("w_s_landed")
        out_stored = sem("out_stored")
        quarters = sem("quarters")
        mix_done = sem("mix_done")
        xt_done = sem("xt_done")
        pt_done = sem("pt_done")
        x1t_done = sem("x1t_done")
        wst_done = sem("wst_done")
        w_hi_ready = sem("w_hi_ready")
        acc_read_act = sem("acc_read_act")
        sigmoid_ready = sem("sigmoid_ready")
        branch_hi_ready = sem("branch_hi_ready")
        v_hi_ready = sem("v_hi_ready")
        small_hi_ready = sem("small_hi_ready")
        squares_done = sem("squares_done")
        w_lo_ready = sem("w_lo_ready")
        acc_read_dve = sem("acc_read_dve")
        small_read = sem("small_read")
        v_norm_ready = sem("v_norm_ready")
        v_lo_ready = sem("v_lo_ready")
        branch_ready = sem("branch_ready")
        branch_lo_ready = sem("branch_lo_ready")
        xn_ready = sem("xn_ready")
        x2_ready = sem("x2_ready")
        y_ready = sem("y_ready")
        rstd_ready = sem("rstd_ready")
        vec_step = sem("vec_step")
        ident_ready = sem("ident_ready")
        masked = sem("masked")
        pool_set = sem("pool_set")

        VEC_PRO, VEC_BLOCK = 23, 96
        EVENTS_PRO, EVENTS = 2, 5

        block = ctx.enter_context(nc.Block())

        def w_source(u):
            kind, a, part = unit_kind(u % UNITS)
            if kind == "V":
                return w_in_k[:, 2 * part:2 * part + 2, COLUMN0["v"]:COLUMN0["v"] + HALF]
            if kind == "T":
                c = COLUMN0[PARTS[part]] + a * P
                return w_in_k[:, :, c:c + P]
            cols = slice(a * HALF, (a + 1) * HALF)
            if kind == "O":
                k = O_CHUNKS[part][0]
                return w_out_k[:, k:k + 2, cols]
            if kind == "P":
                return w_proj_k[:, :, cols]
            return w_gate_k[:, 2 * part:2 * part + 2, cols]

        def w_view(t, u):
            k = KC if unit_kind(u % UNITS)[0] == "T" else 2
            return t[:, u % 2, :].rearrange("p (k n) -> p k n", k=k)

        def quarter(b, u, tile=3):
            return b * Q + 4 * u + tile + 1

        def event(b, e):
            return b * EVENTS + EVENTS_PRO + e + 1

        def over_blocks(eng, body):
            with eng.Fori(0, BLOCKS - 1) as b:
                body(b, False)
            body(BLOCKS - 1, True)

        @block.sync
        def _(sp):
            def load_w(b, u):
                if not (isinstance(b, int) and b == 0 and u < 2):
                    sp.wait_ge(w_lo_ready, b * UNITS + u - 1)
                sp.dma_start(w_view(w_raw, u), w_source(u)).then_inc(w_landed[u % 2], 16)

            sp.sem_inc(out_stored, 16 * TILES)
            for i in range(TILES):
                sp.dma_start(x_res[:, i, :], x_tiles[0, i]).then_inc(x_first_landed[i], 16)
                if i == 1:
                    sp.dma_start(norm_b[:, :], norm_g[0:1, :].to_broadcast([P, d])).then_inc(norm_landed, 16)
            load_w(0, 0)
            load_w(0, 1)
            sp.dma_start(uz[:, 0, :].rearrange("t (h s) -> t h s", h=heads),
                         w_s[0].rearrange("h t s -> t h s")).then_inc(w_s_landed, 16)
            sp.dma_start(uz[:, 1, :], b_s.rearrange("l h t -> l (h t)").to_broadcast([P, heads * P])).then_inc(const_landed, 16)
            load_w(0, 2)
            with nc.allow_non_contiguous_dma(reason="a few hundred parameters, once"):
                sp.dma_start(ln_g_c[:, :], ln_v_g[0].rearrange("(h p) -> p h", p=P)).then_inc(const_landed, 16)
                sp.dma_start(ln_b_c[:, :], ln_v_b[0].rearrange("(h p) -> p h", p=P)).then_inc(const_landed, 16)
                sp.dma_start(conv_c[:, :, :], conv_w[0].rearrange("(h p) k -> p h k", p=P)).then_inc(const_landed, 16)
                sp.dma_start(ple_c[:, :], ple_norm_g[0].rearrange("(k p) -> p k", p=P)).then_inc(const_landed, 16)
            load_w(0, 3)
            sp.dma_start(final_b[:, :], final_g.rearrange("(l n) -> l n", l=1).to_broadcast([P, d])).then_inc(const_landed, 16)
            for u in range(4, 8):
                load_w(0, u)

            def body(b, last):
                for u in range(8, UNITS if last else UNITS + 8):
                    load_w(b, u)
                    if u == 12:
                        sp.wait_ge(out_stored, (b + 1) * (16 * TILES))
                        sp.wait_ge(xt_done, b * 8 + 8)
                        sp.dma_start(x_res[:, :, :], x_block[b]).then_inc(x_res_landed, 16)
                        sp.dma_start(p_nat[:, :, :], p_block[b]).then_inc(p_landed, 16)
                    if u == 8 and not last:
                        for i in (0, 1):
                            sp.wait_ge(xt_done, b * 8 + 6 + 2 * i)
                            sp.dma_start(x_in[:, i, :], x_tiles[b + 1, i]).then_inc(x_in_landed[i], 16)
                    if u in (31, 33) and not last:
                        i = 2 if u == 31 else 3
                        sp.wait_ge(xt_done, b * 8 + 8 + 2 * (i - 1))
                        sp.dma_start(x_in[:, i % 2, :], x_tiles[b + 1, i]).then_inc(x_in_landed[i % 2], 16)
                for i in range(TILES):
                    sp.wait_ge(y_ready, b * TILES + i + 1)
                    sp.dma_start(out_tiles[b, i], x_res[:, i, :]).then_inc(out_stored, 16)

            over_blocks(sp, body)
            sp.wait_ge(out_stored, (BLOCKS + 1) * TILES * 16)

        @block.gpsimd
        def _(pool):
            pool.memset(warm[:, 0:1], 0.0).then_inc(pool_set, 1)
            pool.memset(ident[:, :], 0.0).then_inc(pool_set, 1)
            pool.memset(xc_tail[:, :, :], 0.0).then_inc(pool_set, 1)
            pool.wait_ge(pool_set, 3)
            pool.affine_select(out=ident[:, :], in_=ident[:, :], compare_op=ALU.not_equal, fill=1.0, base=0,
                               pattern=[[-1, P]], channel_multiplier=1).then_inc(ident_ready, 1)

            for u in (0, 1):
                pool.wait_ge(w_hi_ready, u + 1)
                pool.tensor_tensor(w_lo[:, u, :], w_raw[:, u, :], w_hi[:, u, :].bitcast(F32),
                                   ALU.subtract).then_inc(w_lo_ready, 1)
            pool.wait_ge(w_s_landed, 16)
            wsn = uz[:, 0, :].rearrange("t (h s) -> t h s", h=heads)
            pool.affine_select(out=wsn, in_=wsn, compare_op=ALU.is_ge, fill=0.0, base=0,
                               pattern=[[0, heads], [-1, P]], channel_multiplier=1).then_inc(masked, 1)

        @block.tensor
        def _(pe):
            def product(ps, left_hi, left_lo, right_hi, right_lo, first, last):
                pe.matmul(ps, left_hi, right_hi, start=first, stop=False)
                pe.matmul(ps, left_hi, right_lo, start=False, stop=False)
                return pe.matmul(ps, left_lo, right_hi, start=False, stop=last)

            def wait_bank(b, u, n):
                before = [m for m in range(n) if bank_of(m) == bank_of(n)]
                if before:
                    m = before[-1]
                    if unit_of(m) <= u - 3:
                        return
                    if READERS[m] == "act":
                        pe.wait_ge(acc_read_act, b * ACT_READS + reads_through(m))
                    else:
                        pe.wait_ge(acc_read_dve, b * DVE_READS + reads_through(m))
                    return
                m = max(m for m in range(len(READERS)) if bank_of(m) == bank_of(n))
                if unit_of(m) > UNITS + u - 3 and not (isinstance(b, int) and b == 0):
                    pe.wait_ge(acc_read_act, b * ACT_READS + reads_through(m) - ACT_READS)

            def unit(b, u, tiles=range(TILES)):
                kind, a, part = unit_kind(u)
                pe.wait_ge(w_lo_ready, b * UNITS + u + 1)
                hi, lo = w_view(w_hi, u), w_view(w_lo, u)
                if kind == "T":
                    n = acc_index(u, 0)
                    wait_bank(b, u, n)
                    for k in range(KC):
                        ins = product(acc[:, bank_of(n), :], hi[:, k, :], lo[:, k, :],
                                      hn_hi[:, k, :], hn_lo[:, k, :], k == 0, k == KC - 1)
                        if k % 2:
                            ins.then_inc(quarters, 1)
                    return
                left_hi, left_lo, k0, first, last = {
                    "V": (hn_hi, hn_lo, 2 * part, part == 0, part == 3),
                    "O": (mix_hi, mix_lo, O_CHUNKS[part][0], part == 0, part == 3),
                    "P": (pt_hi, pt_lo, 0, True, True),
                    "G": (x1_hi, x1_lo, 2 * part, part == 0, part == 3),
                }[kind]
                for i in tiles:
                    n = acc_index(u, i)
                    if first:
                        wait_bank(b, u, n)
                    for kk in range(2):
                        k, t = k0 + kk, slice(i * P, (i + 1) * P)
                        ins = product(acc[:, bank_of(n), :], left_hi[:, k, t], left_lo[:, k, t],
                                      hi[:, kk, :], lo[:, kk, :], first and kk == 0, last and kk == 1)
                    ins.then_inc(quarters, 1)

            def transposes(bank, sources, done):
                for n, s in enumerate(sources):
                    ins = pe.transpose(small[:, bank, n * P:(n + 1) * P], s, ident[:, :])
                ins.then_inc(done, 1)

            def first_xt(i):
                pe.wait_ge(xn_ready, i + 1)
                for half in range(2):
                    if i:
                        pe.wait_ge(small_read, 2 * i + half - 1)
                    transposes(half, [x_res[:, i, (4 * half + k) * P:(4 * half + k + 1) * P] for k in range(4)], xt_done)

            def first_v(i):
                pe.wait_ge(small_read, 2 * i + 2)
                unit(0, 0, (i,))

            pe.wait_ge(ident_ready, 1)
            first_xt(0)
            first_xt(1)
            first_v(0)
            first_xt(2)
            first_v(1)
            first_xt(3)
            first_v(2)
            pe.wait_ge(masked, 1)
            pe.wait_ge(small_read, 7)
            transposes(0, [uz[:, 0, h * P:(h + 1) * P] for h in range(heads)], wst_done)
            first_v(3)
            pe.wait_ge(small_read, 9)
            pe.matmul(small[:, 1, :], ones_r[:, :], wst_hi, start=True, stop=False)
            pe.matmul(small[:, 1, :], ones_r[:, :], wst_lo, start=False, stop=True).then_inc(wst_done, 1)

            def body(b, last):
                index = {job: n for n, (_, job) in enumerate(jobs_of(last))}

                def small_count(job):
                    return b * JOBS + PRO_JOBS + index[job] + 1

                for u in range(1, UNITS if last else UNITS + 1):
                    if u == UNITS:
                        pe.wait_ge(small_read, b * JOBS + PRO_JOBS + JOBS)
                        unit(b + 1, 0)
                        continue
                    kind, a, part = unit_kind(u)
                    if kind == "O" and a == 0:
                        pe.wait_ge(branch_lo_ready, b * 8 + max(made(k) for k in O_CHUNKS[part]))
                    if kind == "P" and a == 0:
                        pe.wait_ge(small_read, small_count(("pt", 1, 0)))
                    if kind == "G" and a == 0 and part in (0, 2):
                        pe.wait_ge(small_read, small_count(("x1t", 3, part // 2)))
                    unit(b, u)
                    for job in JOBS_AFTER.get(u, ()):
                        if job not in index:
                            continue
                        what, i, half = job
                        n = index[job]
                        both = what == "mix" or (n and jobs_of(last)[n - 1][1][0] == "mix")
                        pe.wait_ge(small_read, b * JOBS + PRO_JOBS + n - (0 if both else 1))
                        if what == "mix":
                            pe.wait_ge(v_lo_ready, b * TILES + TILES)
                            for c in range(TILES):
                                hs = slice(i * P, (i + 1) * P)
                                pe.matmul(mixed[:, c, :, :], x1_hi[:, c, hs], wst[:, i, :, :], start=True, stop=False)
                                ins = pe.matmul(mixed[:, c, 0, :], x1_lo[:, c, hs], wst_hi[:, i, :], start=False, stop=True)
                            ins.then_inc(mix_done, 1)
                        elif what == "xt":
                            pe.wait_ge(xn_ready, b * TILES + TILES + i + 1)
                            xt_bank = n % 2
                            transposes(xt_bank, [x_in[:, i % 2, (4 * half + k) * P:(4 * half + k + 1) * P]
                                                 for k in range(4)], xt_done)
                        elif what == "pt":
                            pe.wait_ge(p_landed, b * 16 + 16)
                            transposes(n % 2, [p_nat[:, t, i * P:(i + 1) * P] for t in range(TILES)], pt_done)
                        else:
                            pe.wait_ge(acc_read_dve, b * DVE_READS + reads_through(28 + 4 * half + i))
                            transposes(n % 2, [x_res[:, i, (4 * half + k) * P:(4 * half + k + 1) * P]
                                               for k in range(4)], x1t_done)

            over_blocks(pe, body)

        @block.scalar
        def _(act):

            def sigmoid_table():
                act.activation(warm[:, 1:2], warm[:, 0:1], ACT.Sigmoid)

            def split_hi(b, u):
                act.wait_ge(w_landed[u % 2], (b * (UNITS // 2) + u // 2 + 1) * 16)
                if not (isinstance(b, int) and b == 0 and u < 2):
                    act.wait_ge(quarters, b * Q + 4 * (u - 1))
                if unit_kind(u % UNITS)[0] == "G":
                    k = 2 * unit_kind(u)[2]
                    for kk in range(2):
                        ins = act.activation(w_view(w_hi, u)[:, kk, :], w_view(w_raw, u)[:, kk, :], ACT.Copy,
                                             scale=ple_c[:, k + kk:k + kk + 1])
                else:
                    ins = act.activation(w_hi[:, u % 2, :], w_raw[:, u % 2, :], ACT.Copy)
                ins.then_inc(w_hi_ready, 1)

            def squares(source, col, done):
                if done is not None:
                    act.wait_ge(squares_done, done)
                act.activation(square[:, :], source, ACT.Square, accum_out=sums[:, col:col + 1]).then_inc(squares_done, 1)

            def mix_part_hi(b, k):
                act.wait_ge(branch_ready, b * 8 + made(k))
                act.activation(mix_hi[:, k, :], branch[:, made(k) % 2, :], ACT.Copy).then_inc(branch_hi_ready, 1)

            def x2_squares(b, last, i):
                act.wait_ge(x2_ready, b * 8 + 4 + i + 1)
                squares(x_res[:, i, :], C_X2 + i, b * 12 + 4 + (4 if last else 8) + i)

            def small_hi(bank, target):
                k = target.shape[1]
                act.activation(target, small[:, bank, :].rearrange("p (k n) -> p k n", k=k),
                               ACT.Copy).then_inc(small_hi_ready, 1)

            def hn_part(t, i, half):
                return t[:, 4 * half:4 * half + 4, i * P:(i + 1) * P]

            act.wait_ge(pool_set, 1)
            sigmoid_table()
            for i in range(TILES):
                act.wait_ge(x_first_landed[i], 16)
                squares(x_res[:, i, :], C_X + i, i or None)
            split_hi(0, 0)
            for i in range(TILES):
                for half in range(2):
                    act.wait_ge(xt_done, 2 * i + half + 1)
                    small_hi(half, hn_part(hn_hi, i, half))
                if i == 1:
                    split_hi(0, 1)
            act.wait_ge(wst_done, 1)
            small_hi(0, wst_hi)
            for u in range(2, 5):
                split_hi(0, u)

            def body(b, last):
                jobs = jobs_of(last)
                sigmoid_table()
                for slot in range(4, 50):
                    if slot not in READ_FIRST and (not last or slot + 1 < UNITS):
                        split_hi(b, slot + 1)
                    kind, a, part = unit_kind(slot - 1) if slot <= UNITS else ("end", 0, 0)
                    if slot == 4:
                        for i in range(TILES):
                            act.wait_ge(quarters, quarter(b, 3, i))
                            act.activation(v_raw[:, i, :], acc[:, bank_of(acc_index(3, i)), :], ACT.Copy).then_inc(acc_read_act, 1)
                    if kind == "T":
                        bank = acc[:, bank_of(acc_index(slot - 1, 0)), :]
                        what = PARTS[part]
                        if what in ("z_a", "z_b"):
                            g = 0 if what == "z_a" else 1
                            act.wait_ge(quarters, quarter(b, slot - 1))
                            if a:
                                if g == 0:
                                    act.wait_ge(acc_read_dve, b * DVE_READS + 5 * (a - 1) + 2)
                                else:
                                    act.wait_ge(branch_ready, b * 8 + made(3 + a))
                            act.activation(gate[:, g, :], bank, ACT.Sigmoid).then_inc(sigmoid_ready, 1)
                        if what == "h":
                            act.wait_ge(quarters, quarter(b, slot - 1))
                            if a:
                                act.wait_ge(acc_read_dve, b * DVE_READS + 5 * (a - 1) + 3)
                            act.activation(h_copy[:, :], bank, ACT.Copy).then_inc(acc_read_act, 1)
                        if v_tile(a, what) is not None:
                            t = v_tile(a, what)
                            act.wait_ge(v_norm_ready, b * TILES + t + 1)
                            act.activation(x1_hi[:, t, :], v_raw[:, t, :], ACT.Copy).then_inc(v_hi_ready, 1)
                        if what == "z_b":
                            mix_part_hi(b, 4 + a)
                    if kind == "P":
                        for i in range(TILES):
                            act.wait_ge(quarters, quarter(b, slot - 1, i))
                            act.activation((uz, v_raw)[a][:, i, :], acc[:, bank_of(acc_index(slot - 1, i)), :],
                                           ACT.Copy).then_inc(acc_read_act, 1)
                    if kind == "G" and part == 3:
                        if a == 0:
                            act.wait_ge(rstd_ready, event(b, 1 if last else 3))
                        for i in range(TILES):
                            act.wait_ge(quarters, quarter(b, slot - 1, i))
                            if 4 * a + i >= 2:
                                act.wait_ge(x2_ready, b * 8 + 4 * a + i - 1)
                            act.activation(gate[:, i % 2, :], acc[:, bank_of(acc_index(slot - 1, i)), :],
                                           ACT.Sigmoid, scale=rstd[:, C_X1 + i:C_X1 + i + 1]).then_inc(acc_read_act, 1)
                            if last and a and i:
                                x2_squares(b, last, i - 1)
                    if slot in READ_FIRST and (not last or slot + 1 < UNITS):
                        split_hi(b, slot + 1)
                    for n, (u, (what, i, half)) in enumerate(jobs):
                        if u != slot - 1:
                            continue
                        if what == "mix":
                            mix_part_hi(b, i)
                        elif what == "xt":
                            act.wait_ge(xt_done, b * 8 + 8 + 2 * i + half + 1)
                            small_hi(n % 2, hn_part(hn_hi, i, half))
                        elif what == "pt":
                            act.wait_ge(pt_done, b * KP + i + 1)
                            small_hi(n % 2, pt_hi[:, i:i + 1, :])
                        else:
                            act.wait_ge(x1t_done, b * 8 + 4 * half + i + 1)
                            small_hi(n % 2, hn_part(x1_hi, i, half))
                    if slot == 10 and not last:
                        for i in (0, 1):
                            act.wait_ge(x_in_landed[i], (b * 2 + 1) * 16)
                            squares(x_in[:, i, :], C_X + i, b * 12 + 4 + i)
                    if slot == 34 and not last:
                        for i in (2, 3):
                            act.wait_ge(x_in_landed[i % 2], (b * 2 + 2) * 16)
                            squares(x_in[:, i % 2, :], C_X + i, b * 12 + 4 + i)
                    if slot in (38, 39):
                        for i in ((0, 1) if slot == 38 else (2, 3)):
                            act.wait_ge(acc_read_dve, b * DVE_READS + 25 + i)
                            squares(x_res[:, i, :], C_X1 + i, b * 12 + 4 + (0 if last else 4) + i)
                    if slot == 47:
                        for i in range(TILES - 1 if last else 0, TILES):
                            x2_squares(b, last, i)

            over_blocks(act, body)

        @block.vector
        def _(dve):
            steps = [0]

            def mark(ins):
                steps[0] += 1
                ins.then_inc(vec_step, 1)

            def step(b, ins):
                mark(ins)
                wait_steps(b)

            def wait_steps(b):
                if b is None:
                    dve.wait_ge(vec_step, steps[0])
                else:
                    dve.wait_ge(vec_step, b * VEC_BLOCK + VEC_PRO + steps[0])

            def split_lo(b, u):
                dve.wait_ge(w_hi_ready, b * UNITS + u + 1)
                if unit_kind(u % UNITS)[0] == "G":
                    k = 2 * unit_kind(u)[2]
                    for kk in range(2):
                        ins = dve.scalar_tensor_tensor(
                            out=w_view(w_lo, u)[:, kk, :], in0=w_view(w_raw, u)[:, kk, :],
                            scalar=ple_c[:, k + kk:k + kk + 1], in1=w_view(w_hi, u)[:, kk, :].bitcast(F32),
                            op0=ALU.mult, op1=ALU.subtract)
                else:
                    ins = dve.tensor_tensor(w_lo[:, u % 2, :], w_raw[:, u % 2, :],
                                            w_hi[:, u % 2, :].bitcast(F32), ALU.subtract)
                ins.then_inc(w_lo_ready, 1)

            def mix_part_lo(b, k):
                dve.wait_ge(branch_ready, b * 8 + made(k))
                dve.wait_ge(branch_hi_ready, b * 8 + made(k))
                dve.tensor_tensor(mix_lo[:, k, :], branch[:, made(k) % 2, :], mix_hi[:, k, :].bitcast(F32),
                                  ALU.subtract).then_inc(branch_lo_ready, 1)

            def small_lo(bank, hi, lo):
                k = lo.shape[1]
                dve.tensor_tensor(lo, small[:, bank, :].rearrange("p (k n) -> p k n", k=k),
                                  hi.bitcast(F32), ALU.subtract).then_inc(small_read, 1)

            def hn_part(t, i, half):
                return t[:, 4 * half:4 * half + 4, i * P:(i + 1) * P]

            def mean_squares(b, c0, c1):
                step(b, dve.tensor_scalar(var[:, c0:c1], sums[:, c0:c1], 1.0 / d, EPS, ALU.mult, ALU.add))

            def rsqrt(b, c0, c1):
                y, v, t = (m[:, c0:c1] for m in (rstd, var, newton))
                step(b, dve.tensor_scalar(shifted[:, c0:c1], v.bitcast(I32), 1, None, ALU.logical_shift_right))
                step(b, dve.tensor_scalar(y.bitcast(I32), shifted[:, c0:c1], -1.0, float(RSQRT_MAGIC),
                                          ALU.mult, ALU.add))
                for r in range(NEWTON_ROUNDS):
                    step(b, dve.scalar_tensor_tensor(out=t, in0=y, scalar=-0.5, in1=y, op0=ALU.mult, op1=ALU.mult))
                    step(b, dve.tensor_tensor(t, t, v, ALU.mult))
                    ins = dve.scalar_tensor_tensor(out=y, in0=t, scalar=1.5, in1=y, op0=ALU.add, op1=ALU.mult)
                    if r < NEWTON_ROUNDS - 1:
                        step(b, ins)
                ins.then_inc(rstd_ready, 1)

            def normalise_x(tile, i):
                dve.scalar_tensor_tensor(out=tile, in0=tile, scalar=rstd[:, C_X + i:C_X + i + 1], in1=norm_b[:, :],
                                         op0=ALU.mult, op1=ALU.mult).then_inc(xn_ready, 1)

            def first_lo(i):
                for half in range(2):
                    dve.wait_ge(small_hi_ready, 2 * i + half + 1)
                    small_lo(half, hn_part(hn_hi, i, half), hn_part(hn_lo, i, half))

            step(None, dve.memset(ones_r[:, :].bitcast(F32), 1.0))
            for pair in range(2):
                c0 = C_X + 2 * pair
                dve.wait_ge(squares_done, 2 * pair + 2)
                mean_squares(None, c0, c0 + 2)
                rsqrt(None, c0, c0 + 2)
                if pair == 0:
                    dve.wait_ge(norm_landed, 16)
                    dve.wait_ge(rstd_ready, 1)
                    normalise_x(x_res[:, 0, :], 0)
                    normalise_x(x_res[:, 1, :], 1)
            dve.wait_ge(rstd_ready, 2)
            first_lo(0)
            normalise_x(x_res[:, 2, :], 2)
            first_lo(1)
            normalise_x(x_res[:, 3, :], 3)
            first_lo(2)
            first_lo(3)
            dve.wait_ge(w_lo_ready, 2)
            dve.wait_ge(small_hi_ready, 9)
            small_lo(0, wst_hi, wst_lo)
            for u in range(2, 5):
                split_lo(0, u)
                if u == 2:
                    dve.wait_ge(wst_done, 2)
                    dve.wait_ge(const_landed, 16 * 6)
                    for h in range(heads):
                        ins = dve.scalar_tensor_tensor(
                            out=mix_add[:, h, :], in0=small[:, 1, h * P:(h + 1) * P], scalar=ln_b_c[:, h:h + 1],
                            in1=uz[:, 1, h * P:(h + 1) * P], op0=ALU.mult, op1=ALU.add)
                    ins.then_inc(small_read, 1)
            assert steps[0] == VEC_PRO

            PRO_HI, HI_JOBS = 9, JOBS - heads

            def body(b, last):
                steps[0] = 0
                jobs = jobs_of(last)
                for slot in range(4, 50):
                    if slot not in READ_FIRST and (not last or slot + 1 < UNITS):
                        split_lo(b, slot + 1)
                    kind, a, part = unit_kind(slot - 1) if slot <= UNITS else ("end", 0, 0)
                    if slot == 4:
                        for i in range(TILES):
                            dve.wait_ge(acc_read_act, b * ACT_READS + i + 1)
                            if i:
                                wait_steps(b)
                            mark(dve.bn_stats(bn[:, i, :], v_raw[:, i, :]))
                            if i:
                                mark(dve.bn_aggr(mean_var[:, i - 1, :], bn[:, i - 1, :]))
                        wait_steps(b)
                        mark(dve.tensor_scalar(var[:, C_V:C_V + 3], mean_var[:, 0:3, 1], EPS, None, ALU.add))
                        mark(dve.bn_aggr(mean_var[:, 3, :], bn[:, 3, :]))
                        wait_steps(b)
                        step(b, dve.tensor_scalar(var[:, C_V + 3:C_V + 4], mean_var[:, 3:4, 1], EPS, None, ALU.add))
                        rsqrt(b, C_V, C_V + 4)
                    if kind == "T":
                        bank = acc[:, bank_of(acc_index(slot - 1, 0)), :]
                        reads = b * DVE_READS + 5 * a
                        what = PARTS[part]
                        if what != "h":
                            dve.wait_ge(quarters, quarter(b, slot - 1))
                        if what == "z_a":
                            dve.wait_ge(sigmoid_ready, b * 8 + 2 * a + 1)
                            dve.tensor_tensor(gate[:, 0, :], bank, gate[:, 0, :], ALU.mult).then_inc(acc_read_dve, 1)
                        if what == "u":
                            dve.wait_ge(acc_read_dve, reads + 1)
                            dve.tensor_tensor(uz[:, a, :], bank, gate[:, 0, :], ALU.mult).then_inc(acc_read_dve, 1)
                        if v_tile(a, what) is not None:
                            t = v_tile(a, what)
                            if t == 0:
                                dve.wait_ge(rstd_ready, event(b, 0))
                            dve.tensor_scalar(v_raw[:, t, :], v_raw[:, t, :], mean_var[:, t, 0:1],
                                              rstd[:, C_V + t:C_V + t + 1], ALU.subtract, ALU.mult).then_inc(v_norm_ready, 1)
                            dve.wait_ge(v_norm_ready, b * TILES + t + 1)
                            dve.wait_ge(v_hi_ready, b * TILES + t + 1)
                            dve.tensor_tensor(x1_lo[:, t, :], v_raw[:, t, :], x1_hi[:, t, :].bitcast(F32),
                                              ALU.subtract).then_inc(v_lo_ready, 1)
                        if what == "gate_c":
                            step(b, dve.tensor_copy(xc[:, 0:2], xc_tail[:, a, :]))
                            dve.wait_ge(acc_read_act, b * ACT_READS + 4 + a + 1)
                            dve.tensor_tensor(xc[:, 2:], bank, h_copy[:, :], ALU.mult).then_inc(acc_read_dve, 1)
                            dve.wait_ge(acc_read_dve, reads + 3)
                            step(b, dve.tensor_scalar(conv[:, :], xc[:, 0:HALF], conv_c[:, a, 0:1], None, ALU.mult))
                            for k in (1, 2):
                                step(b, dve.scalar_tensor_tensor(out=conv[:, :], in0=xc[:, k:k + HALF],
                                                                 scalar=conv_c[:, a, k:k + 1], in1=conv[:, :],
                                                                 op0=ALU.mult, op1=ALU.add))
                            step(b, dve.tensor_copy(xc_tail[:, a, :], xc[:, HALF:HALF + 2]))
                        if what == "gate_b":
                            dve.tensor_tensor(conv[:, :], bank, conv[:, :], ALU.mult).then_inc(acc_read_dve, 1)
                        if what == "z_b":
                            dve.wait_ge(sigmoid_ready, b * 8 + 2 * a + 2)
                            dve.tensor_tensor(gate[:, 1, :], bank, gate[:, 1, :], ALU.mult).then_inc(acc_read_dve, 1)
                            dve.wait_ge(acc_read_dve, reads + 5)
                            dve.tensor_tensor(branch[:, made(4 + a) % 2, :], gate[:, 1, :], conv[:, :],
                                              ALU.mult).then_inc(branch_ready, 1)
                            mix_part_lo(b, 4 + a)
                    if kind == "O" and part == 3:
                        if a == 0:
                            dve.wait_ge(x_res_landed, b * 16 + 16)
                        for i in range(TILES):
                            dve.wait_ge(quarters, quarter(b, slot - 1, i))
                            xh = x_res[:, i, a * HALF:(a + 1) * HALF]
                            dve.tensor_tensor(xh, acc[:, bank_of(acc_index(slot - 1, i)), :], xh, ALU.add).then_inc(acc_read_dve, 1)
                    if kind == "G" and part == 3:
                        for i in range(TILES):
                            dve.wait_ge(acc_read_act, b * ACT_READS + 12 + 8 * a + i + 1)
                            pp = (uz, v_raw)[a][:, i, :]
                            step(b, dve.tensor_tensor(pp, gate[:, i % 2, :], pp, ALU.mult))
                            xh = x_res[:, i, a * HALF:(a + 1) * HALF]
                            dve.tensor_tensor(xh, pp, xh, ALU.add).then_inc(x2_ready, 1)
                    if slot in READ_FIRST and (not last or slot + 1 < UNITS):
                        split_lo(b, slot + 1)
                    hi_jobs = 0
                    for n, (u, (what, i, half)) in enumerate(jobs):
                        if u == slot - 1:
                            if what == "mix":
                                br = branch[:, made(i) % 2, :]
                                br_c = br.rearrange("p (c t) -> p c t", c=TILES)
                                dve.wait_ge(mix_done, b * heads + i + 1)
                                step(b, dve.scalar_tensor_tensor(
                                    out=br_c, in0=mixed[:, :, 0, :], scalar=ln_g_c[:, i:i + 1],
                                    in1=mix_add[:, i:i + 1, :].to_broadcast([P, TILES, P]), op0=ALU.mult, op1=ALU.add))
                                dve.scalar_tensor_tensor(
                                    out=br_c, in0=mixed[:, :, 1, :], scalar=ln_g_c[:, i:i + 1],
                                    in1=br_c, op0=ALU.mult, op1=ALU.add).then_inc(small_read, 1)
                                dve.wait_ge(small_read, b * JOBS + PRO_JOBS + n + 1)
                                dve.tensor_tensor(br, br, uz[:, i, :], ALU.mult).then_inc(branch_ready, 1)
                                mix_part_lo(b, i)
                            else:
                                dve.wait_ge(small_hi_ready, b * HI_JOBS + PRO_HI + hi_jobs + 1)
                                if what == "pt":
                                    small_lo(n % 2, pt_hi[:, i:i + 1, :], pt_lo[:, i:i + 1, :])
                                else:
                                    th, tl = (hn_hi, hn_lo) if what == "xt" else (x1_hi, x1_lo)
                                    small_lo(n % 2, hn_part(th, i, half), hn_part(tl, i, half))
                        if what != "mix":
                            hi_jobs += 1
                    if not last:
                        if slot in (11, 35):
                            c0 = C_X if slot == 11 else C_X + 2
                            dve.wait_ge(squares_done, b * 12 + 4 + (2 if slot == 11 else 4))
                            mean_squares(b, c0, c0 + 2)
                            rsqrt(b, c0, c0 + 2)
                        for i in {17: (0,), 23: (1,), 39: (2,), 40: (3,)}.get(slot, ()):
                            if i in (0, 2):
                                dve.wait_ge(rstd_ready, event(b, 1 + i // 2))
                            normalise_x(x_in[:, i % 2, :], i)
                    if slot == 40:
                        dve.wait_ge(squares_done, b * 12 + 4 + (4 if last else 8))
                        mean_squares(b, C_X1, C_X1 + 4)
                        rsqrt(b, C_X1, C_X1 + 4)
                    if slot == 47:
                        dve.wait_ge(squares_done, b * 12 + 4 + (8 if last else 12))
                        mean_squares(b, C_X2, C_X2 + 4)
                        rsqrt(b, C_X2, C_X2 + 4)
                    if slot == 49:
                        dve.wait_ge(rstd_ready, event(b, 2 if last else 4))
                        for i in range(TILES):
                            dve.scalar_tensor_tensor(out=x_res[:, i, :], in0=x_res[:, i, :],
                                                     scalar=rstd[:, C_X2 + i:C_X2 + i + 1], in1=final_b[:, :],
                                                     op0=ALU.mult, op1=ALU.mult).then_inc(y_ready, 1)
                if not last:
                    assert steps[0] == VEC_BLOCK, steps[0]

            over_blocks(dve, body)


_INS = ["x", "p", "norm_g", "w_in", "ln_v_g", "ln_v_b", "w_s", "b_s", "conv_w", "w_out", "ple_norm_g",
        "w_ple_gate", "w_ple_proj", "final_g"]


def kernel(**inputs):
    import numpy as _np
    import concourse.bacc as _bacc
    from concourse import mybir as _mybir
    from concourse.bass_utils import run_bass_kernel_spmd as _run

    nc = _bacc.Bacc("TRN2", target_bir_lowering=False, num_devices=1)
    arrays, args = {}, []
    for name in _INS:
        a = _np.ascontiguousarray(inputs[name])
        arrays[f"in_{name}_dram"] = a
        args.append(nc.dram_tensor(f"in_{name}_dram", a.shape, _mybir.dt.from_np(a.dtype), kind="ExternalInput").ap())
    out = nc.dram_tensor("out_dram", inputs["x"].shape, _mybir.dt.float32, kind="ExternalOutput").ap()
    build(nc, *args, out)
    r = _run(nc, [arrays], core_ids=[0])
    return r.results[0]["out_dram"]
```
